# Optimizing a Trainium2 kernel written in Bass

```python
import jax, jax.numpy as jnp
from jax import lax
import numpy as np

D_MODEL = 1024
BATCH = 1
SEQ = 1024
DEPTH = 2

N_MIXERS = 2
N_LRU_LAYERS = (DEPTH + N_MIXERS - 1) // N_MIXERS
N_ATTN_LAYERS = DEPTH // N_MIXERS
N_META = 16
GRID_W = 64
RMS_EPS = 1e-6

D_RNN = D_MODEL
LRU_BLOCKS = 8
LRU_BLOCK_W = D_RNN // LRU_BLOCKS
CONV_W = 4
CONV_PAD_LEFT = 2
LRU_C = 8.0

HEAD_DIM = 128
N_HEADS = D_MODEL // HEAD_DIM
N_KV_HEADS = 2
GQA_GROUP = N_HEADS // N_KV_HEADS
ROPE_AXIS_DIM = HEAD_DIM // 2
ROPE_PAIRS = ROPE_AXIS_DIM // 2
ROPE_THETA = 10000.0
Q_BLOCK = 128
QKV_DIM = (N_HEADS + 2 * N_KV_HEADS) * HEAD_DIM

D_FF = -(-(8 * D_MODEL) // (3 * 256)) * 256

kernel_name = "bidir_hybrid_rglru_axial_gqa_swiglu"

def _rmsnorm(x, g):
    xf = x.astype(jnp.float32)
    y = xf * lax.rsqrt(jnp.mean(xf * xf, axis=-1, keepdims=True) + RMS_EPS)
    return (y * g.astype(jnp.float32)).astype(x.dtype)

def _linear_scan(a, b):
    def combine(left, right):
        a_l, b_l = left
        a_r, b_r = right
        return a_l * a_r, a_r * b_l + b_r
    _, h = lax.associative_scan(combine, (a, b), axis=1)
    return h

def _rglru_direction(u, gate_w, gate_b, lam):
    B, L, _ = u.shape
    ub = u.reshape(B, L, LRU_BLOCKS, LRU_BLOCK_W)
    g = jnp.einsum('blnc,gncd->gblnd', ub, gate_w).reshape(2, B, L, D_RNN)
    g = jax.nn.sigmoid(g.astype(jnp.float32) + gate_b.astype(jnp.float32)[:, None, None, :])
    r, i = g[0], g[1]
    log_a = -LRU_C * r * jax.nn.softplus(-lam.astype(jnp.float32))
    a = jnp.exp(log_a)
    b = jnp.sqrt(-jnp.expm1(2.0 * log_a)) * (i * u.astype(jnp.float32))
    return _linear_scan(a, b)

def _rglru_mixer(h, w_in, conv_w, conv_b, gate_w, gate_b, lam, w_out):
    L = h.shape[1]
    proj = h @ w_in
    y_branch = jax.nn.gelu(proj[..., :D_RNN])
    x_branch = proj[..., D_RNN:]
    xp = jnp.pad(x_branch, ((0, 0), (CONV_PAD_LEFT, CONV_W - 1 - CONV_PAD_LEFT), (0, 0)))
    xc = conv_b
    for k in range(CONV_W):
        xc = xc + xp[:, k:k + L] * conv_w[k]
    fwd = _rglru_direction(xc, gate_w[0], gate_b[0], lam[0])
    bwd = jnp.flip(_rglru_direction(jnp.flip(xc, axis=1), gate_w[1], gate_b[1], lam[1]), axis=1)
    rec = (fwd + bwd).astype(h.dtype)
    return (rec * y_branch) @ w_out

def _axial_rope_angles(n_tokens):
    rows = n_tokens // GRID_W
    inv_freq = ROPE_THETA ** (-jnp.arange(0, ROPE_AXIS_DIM, 2, dtype=jnp.float32) / ROPE_AXIS_DIM)
    ang_r = jnp.arange(rows, dtype=jnp.float32)[:, None] * inv_freq
    ang_c = jnp.arange(GRID_W, dtype=jnp.float32)[:, None] * inv_freq
    ang = jnp.stack([jnp.broadcast_to(ang_r[:, None, :], (rows, GRID_W, ROPE_PAIRS)),
                     jnp.broadcast_to(ang_c[None, :, :], (rows, GRID_W, ROPE_PAIRS))], axis=2)
    ang = ang.reshape(rows * GRID_W, 2, ROPE_PAIRS)
    ang = jnp.concatenate([jnp.zeros((N_META, 2, ROPE_PAIRS), jnp.float32), ang], axis=0)
    return jnp.cos(ang), jnp.sin(ang)

def _apply_rope(x, cos, sin):
    xs = x.reshape(*x.shape[:-1], 2, 2, ROPE_PAIRS)
    x1, x2 = xs[..., 0, :], xs[..., 1, :]
    c = cos.astype(x.dtype)[None, :, None]
    s = sin.astype(x.dtype)[None, :, None]
    out = jnp.stack([x1 * c - x2 * s, x2 * c + x1 * s], axis=-2)
    return out.reshape(x.shape)

def _attn_block(qb, k, v):
    s = jnp.einsum('bqkgd,bskd->bkgqs', qb, k).astype(jnp.float32)
    p = jax.nn.softmax(s, axis=-1).astype(v.dtype)
    return jnp.einsum('bkgqs,bskd->bqkgd', p, v)

def _attention_mixer(h, w_qkv, q_gain, k_gain, w_out, cos, sin):
    B, L, _ = h.shape
    qkv = h @ w_qkv
    q = qkv[..., :N_HEADS * HEAD_DIM].reshape(B, L, N_HEADS, HEAD_DIM)
    k = qkv[..., N_HEADS * HEAD_DIM:(N_HEADS + N_KV_HEADS) * HEAD_DIM].reshape(B, L, N_KV_HEADS, HEAD_DIM)
    v = qkv[..., (N_HEADS + N_KV_HEADS) * HEAD_DIM:].reshape(B, L, N_KV_HEADS, HEAD_DIM)
    q = _apply_rope(_rmsnorm(q, q_gain), cos, sin) * (HEAD_DIM ** -0.5)
    k = _apply_rope(_rmsnorm(k, k_gain), cos, sin)
    q = q.reshape(B, L, N_KV_HEADS, GQA_GROUP, HEAD_DIM)
    out_meta = _attn_block(q[:, :N_META], k, v)
    n_blk = (L - N_META) // Q_BLOCK
    q_real = q[:, N_META:].reshape(B, n_blk, Q_BLOCK, N_KV_HEADS, GQA_GROUP, HEAD_DIM)
    q_real = q_real.transpose(1, 0, 2, 3, 4, 5)
    out_real = lax.map(lambda qb: _attn_block(qb, k, v), q_real)
    out_real = out_real.transpose(1, 0, 2, 3, 4, 5).reshape(B, L - N_META, N_KV_HEADS, GQA_GROUP, HEAD_DIM)
    o = jnp.concatenate([out_meta, out_real], axis=1).reshape(B, L, N_HEADS * HEAD_DIM)
    return o @ w_out

def _swiglu(h, w_in, w_out):
    gu = h @ w_in
    return (jax.nn.silu(gu[..., :D_FF]) * gu[..., D_FF:]) @ w_out

def setup_inputs(seed: int = 0) -> dict:
    key = jax.random.key(seed)
    ks = jax.random.split(key, 18)
    f32 = jnp.float32
    nrm = lambda k, shape, fan_in: jax.random.normal(k, shape, f32) * (fan_in ** -0.5)
    x = jax.random.normal(ks[0], (BATCH, SEQ, D_MODEL), f32)
    meta_tokens = jax.random.normal(ks[1], (N_META, D_MODEL), f32)
    norm_gains = 1.0 + 0.02 * jax.random.normal(ks[2], (DEPTH, 4, D_MODEL), f32)
    lru_w_in = nrm(ks[3], (N_LRU_LAYERS, D_MODEL, 2 * D_RNN), D_MODEL)
    lru_conv_w = nrm(ks[4], (N_LRU_LAYERS, CONV_W, D_RNN), CONV_W)
    lru_conv_b = 0.01 * jax.random.normal(ks[5], (N_LRU_LAYERS, D_RNN), f32)
    lru_gate_w = nrm(ks[6], (N_LRU_LAYERS, 2, 2, LRU_BLOCKS, LRU_BLOCK_W, LRU_BLOCK_W), LRU_BLOCK_W)
    lru_gate_b = 0.01 * jax.random.normal(ks[7], (N_LRU_LAYERS, 2, 2, D_RNN), f32)
    a_c = jax.random.uniform(ks[8], (N_LRU_LAYERS, 2, D_RNN), f32, 0.9, 0.999)
    s = a_c ** (1.0 / LRU_C)
    lru_lambda = jnp.log(s) - jnp.log1p(-s)
    lru_w_out = nrm(ks[9], (N_LRU_LAYERS, D_RNN, D_MODEL), D_RNN)
    attn_w_qkv = nrm(ks[10], (N_ATTN_LAYERS, D_MODEL, QKV_DIM), D_MODEL)
    attn_q_gain = 1.0 + 0.02 * jax.random.normal(ks[11], (N_ATTN_LAYERS, HEAD_DIM), f32)
    attn_k_gain = 1.0 + 0.02 * jax.random.normal(ks[12], (N_ATTN_LAYERS, HEAD_DIM), f32)
    attn_w_out = nrm(ks[13], (N_ATTN_LAYERS, N_HEADS * HEAD_DIM, D_MODEL), N_HEADS * HEAD_DIM)
    ffn_w_in = nrm(ks[14], (DEPTH, D_MODEL, 2 * D_FF), D_MODEL)
    ffn_w_out = nrm(ks[15], (DEPTH, D_FF, D_MODEL), D_FF)
    return {"x": x, "meta_tokens": meta_tokens, "norm_gains": norm_gains,
            "lru_w_in": lru_w_in, "lru_conv_w": lru_conv_w, "lru_conv_b": lru_conv_b,
            "lru_gate_w": lru_gate_w, "lru_gate_b": lru_gate_b, "lru_lambda": lru_lambda,
            "lru_w_out": lru_w_out, "attn_w_qkv": attn_w_qkv, "attn_q_gain": attn_q_gain,
            "attn_k_gain": attn_k_gain, "attn_w_out": attn_w_out,
            "ffn_w_in": ffn_w_in, "ffn_w_out": ffn_w_out}

def reference(x, meta_tokens, norm_gains, lru_w_in, lru_conv_w, lru_conv_b, lru_gate_w,
              lru_gate_b, lru_lambda, lru_w_out, attn_w_qkv, attn_q_gain, attn_k_gain,
              attn_w_out, ffn_w_in, ffn_w_out):
    B, S, _ = x.shape
    meta = jnp.broadcast_to(meta_tokens.astype(x.dtype)[None], (B, N_META, D_MODEL))
    h = jnp.concatenate([meta, x], axis=1)
    cos, sin = _axial_rope_angles(S)
    for layer in range(DEPTH):
        g = norm_gains[layer]
        slot = layer // N_MIXERS
        u = _rmsnorm(h, g[0])
        if layer % N_MIXERS == 0:
            m = _rglru_mixer(u, lru_w_in[slot], lru_conv_w[slot], lru_conv_b[slot],
                             lru_gate_w[slot], lru_gate_b[slot], lru_lambda[slot], lru_w_out[slot])
        else:
            m = _attention_mixer(u, attn_w_qkv[slot], attn_q_gain[slot], attn_k_gain[slot],
                                 attn_w_out[slot], cos, sin)
        h = h + _rmsnorm(m, g[1])
        u = _rmsnorm(h, g[2])
        h = h + _rmsnorm(_swiglu(u, ffn_w_in[layer], ffn_w_out[layer]), g[3])
    return h[:, N_META:]


_drawn_inputs = setup_inputs


def setup_inputs(seed=0):
    import zlib

    import numpy as np

    out = dict(_drawn_inputs(seed))
    spreads = {}
    factors = {'lru_gate_b': 8.0, 'attn_q_gain': 8.0, 'attn_k_gain': 8.0}
    for name, (base, spread) in spreads.items():
        noise = np.random.default_rng([zlib.crc32(name.encode()), seed]).standard_normal(out[name].shape)
        drawn = base * np.exp(spread * noise) if base else spread * noise
        out[name] = __import__('jax').numpy.asarray(drawn.astype(out[name].dtype))
    for name, factor in factors.items():
        out[name] = (out[name] * factor).astype(out[name].dtype)
    return out
```

```python
from contextlib import ExitStack, contextmanager

import numpy as np

import concourse.bass as bass
from concourse import mybir

ALU = mybir.AluOpType
ACT = mybir.ActivationFunctionType
AX_X = mybir.AxisListType.X
F32 = mybir.dt.float32
F32R = mybir.dt.float32r

P = 128
D_MODEL = 1024
F = D_MODEL // P
N_META, SEQ = 16, 1024
REAL = N_META + SEQ
CHUNKS = 3
CW = 348
TOKENS = CHUNKS * CW
PAD = TOKENS - REAL
EPS = 1e-6
D_FF = 2816
FF = D_FF // P
LRU_C = 8.0
CONV_W, CONV_LEFT = 4, 2
HEADS, KV_HEADS = 8, 2
GROUP = HEADS // KV_HEADS
HEAD_DIM = 128
QT = 9
QW = TOKENS // QT
UNIT = 1024
WRING = 3

GAIN = 0
CONVW = GAIN + 2 * 4 * F
CONVB = CONVW + CONV_W * F
GATEB = CONVB + F
LAM = GATEB + 4 * F
QGAIN = LAM + 2 * F
KGAIN = QGAIN + 1
PARAMS = KGAIN + 1

U_LRU = 0
U_LRU_OUT = U_LRU + 3 * F
U_FFN0 = U_LRU_OUT + F
FFN_UNITS = 3 * FF
U_QKV = U_FFN0 + FFN_UNITS
U_ATT_OUT = U_QKV + HEADS + 2 * KV_HEADS
U_FFN1 = U_ATT_OUT + F
UNITS = U_FFN1 + FFN_UNITS

FFN_JOBS = 2 * FF + (FF // 2) * F
VJOBS = QT // 3
J_LRU = 0
J_LRU_OUT = J_LRU + 6 * F
J_FFN0 = J_LRU_OUT + F
J_QKV = J_FFN0 + FFN_JOBS
J_ATT = J_QKV + HEADS + KV_HEADS + VJOBS
J_ATT_OUT = J_ATT + QT * HEADS
J_FFN1 = J_ATT_OUT + F

ATT_AUX = HEADS * 3 + KV_HEADS
A_T0 = 0
A_T1 = A_T0 + CHUNKS
A_T2 = A_T1 + 2 * CHUNKS
A_QKV = A_T2 + 2 * CHUNKS
A_ATT = A_QKV + (HEADS + KV_HEADS) * CHUNKS
A_T3 = A_ATT + QT * ATT_AUX
A_T4 = A_T3 + 2 * CHUNKS


def ring(n, size, i=None, per=0):
    assert per % size == 0
    return n % size, n // size + (0 if i is None else i * (per // size))


def main(n, i=None, per=0):
    return ring(n, 2, i, per)


def aux(n, i=None, per=0):
    return ring(n, 2, i, per)


def wait(eng, sem, value):
    if not isinstance(value, int) or value > 0:
        eng.wait_ge(sem, value)


class Steps:

    def __init__(self, sem, names, base=0):
        self.sem, self.names, self.base, self.at = sem, list(names), base, 0

    def after(self, name, i=0):
        return self.base + self.names.index(name) + 1 + len(self.names) * i

    def did(self, name, instruction):
        assert self.names[self.at % len(self.names)] == name, (name, self.names[self.at % len(self.names)])
        self.at += 1
        instruction.then_inc(self.sem, 1)


def trunk(nc, h0, params, rope, weights, out, spill):
    with ExitStack() as ctx:
        made = {}

        def sem(name):
            made[name] = ctx.enter_context(nc.semaphore(name))
            return made[name]

        def keep(name, shape, dt):
            return ctx.enter_context(nc.sbuf_tensor(name, shape, dt))

        @contextmanager
        def overlay():
            with ExitStack() as own:
                yield lambda name, shape, dt: own.enter_context(nc.sbuf_tensor(name, shape, dt))

        prm = keep("prm", [P, PARAMS], F32)
        ones = keep("ones", [P, P], F32)
        ident = keep("ident", [P, P], F32)
        eps = keep("eps", [P, 1], F32)
        sp = keep("softplus", [P, 6, 2 * F], F32)
        stat = keep("stat", [P, 2, 8], F32)
        raw = keep("raw", [P, WRING, UNIT], F32)
        whi = keep("whi", [P, WRING, UNIT], F32R)
        wlo = keep("wlo", [P, WRING, UNIT], F32R)

        fr, rr = [], []
        for n in range(4):
            with overlay() as sb:
                fr.append(sb(f"region{n}", [P, F, TOKENS], F32))
            rr.append(keep(f"region{n}r", [P, F, TOKENS], F32R))

        with overlay() as sb:
            squares = sb("squares", [P, F, CW], F32)
            scaled = sb("scaled", [P, F, CW], F32)
            root = sb("root", [P, CHUNKS, CW], F32)
            rstd = sb("rstd", [P, CHUNKS, CW], F32)
            sumsq = sb("sumsq", [P, TOKENS], F32)
            sqtile = sb("sqtile", [P, TOKENS], F32)
        with overlay() as sb:
            xpad = sb("xpad", [P, TOKENS + CONV_W - 1], F32)
            xc = sb("xc", [P, TOKENS], F32)
            xch = sb("xch", [P, TOKENS], F32R)
            xcl = sb("xcl", [P, TOKENS], F32R)
        with ExitStack() as att:
            vlo = att.enter_context(nc.sbuf_tensor("vlo", [P, QT, KV_HEADS * HEAD_DIM], F32R))
            with overlay() as sb:
                cossin = sb("cossin", [P, 2, TOKENS], F32)
                hg = sb("hg", [P, TOKENS], F32)
                hs = sb("hs", [P, TOKENS], F32)
                hsq = sb("hsq", [P, TOKENS], F32)
                hroot = sb("hroot", [P, CHUNKS, CW], F32)
                hrstd = sb("hrstd", [P, CHUNKS, CW], F32)
            with overlay() as sb:
                prob = sb("prob", [P, 2, TOKENS], F32)
                qsh = sb("qsh", [P, HEADS, QW], F32R)
                qsl = sb("qsl", [P, HEADS, QW], F32R)

        slots = [ctx.enter_context(nc.psum_tensor(f"slot{s}", [P, CHUNKS, 512], F32)) for s in range(2)]
        banks = [ctx.enter_context(nc.psum_tensor(f"bank{s}", [P, 512], F32)) for s in range(2)]

        main_full = [sem(f"main_full{s}") for s in range(2)]
        main_free = [sem(f"main_free{s}") for s in range(2)]
        aux_full = [sem(f"aux_full{s}") for s in range(2)]
        aux_free = [sem(f"aux_free{s}") for s in range(2)]
        raw_full = [sem(f"raw_full{s}") for s in range(WRING)]
        split_begun, hi_done = sem("split_begun"), sem("hi_done")
        w_ready = [sem(f"w_ready{s}") for s in range(WRING)]
        w_free = [sem(f"w_free{s}") for s in range(WRING)]
        loaded = sem("loaded")
        tables_in = sem("tables_in")
        const_ready = sem("const_ready")
        h_spilled, h_back, out_done = sem("h_spilled"), sem("h_back"), sem("out_done")

        sp_v = Steps(sem("sp_v"), [f"s{n}" for n in range(23)])
        sp_a = Steps(sem("sp_a"), ["exp"])

        def norm_steps(tag, has_m, has_u):
            v, a, g = [], [], []
            order = (["A0", "B0", "A1", "B1", "A2", "B2"] if False else ["A0", "A1", "B0", "A2", "B1", "B2"])
            for what in order:
                k, c = what[0], what[1]
                if k == "A" and has_m:
                    v += [f"rm{c}", f"mr{c}"] + [f"h{c}_{f}" for f in range(F)]
                if k == "B" and has_u:
                    v += [f"rh{c}"] + [f"u{c}_{f}" for f in range(F)]
            for what in ["sq0", "sq1", "hi0", "sq2", "hi1", "hi2"]:
                if has_u:
                    a.append(what)
            g = [f"lo{c}" for c in range(CHUNKS)] if has_u else []
            return (Steps(sem(f"{tag}_v"), v) if v else None, Steps(sem(f"{tag}_a"), a) if a else None,
                    Steps(sem(f"{tag}_g"), g) if g else None)

        t_steps = [norm_steps("t0", False, True), norm_steps("t1", True, True), norm_steps("t2", True, True),
                   norm_steps("t3", True, True), norm_steps("t4", True, False)]

        lru_vn = ["tap1", "tap2", "tap3", "xc_lo", "ix0", "ix1", "q0", "q1", "b0", "scan0", "b1", "scan1", "rec", "z"]
        lru_an = ["tap0", "xc_hi", "a0", "a1", "t0", "t1", "sq0", "sq1", "root0", "root1"]
        lru_v = Steps(sem("lru_v"), lru_vn, base=len(lru_vn))
        lru_a = Steps(sem("lru_a"), lru_an)

        def out_steps(tag):
            return (Steps(sem(f"{tag}_split_v"), ["lo"]), Steps(sem(f"{tag}_split_a"), ["hi"]),
                    Steps(sem(f"{tag}_v"), [f"sum{m}" for m in range(1, F)]),
                    Steps(sem(f"{tag}_a"), [f"copy{m}" for m in range(F)]))

        out_st = [out_steps("lo0"), out_steps("lo1")]

        def ffn_steps(tag):
            return (Steps(sem(f"{tag}_v"), ["lo_a", "lo_b"]), Steps(sem(f"{tag}_a"), ["hi_a", "hi_b"]),
                    Steps(sem(f"{tag}_sv"), [f"sum{m}" for m in range(1, F)]),
                    Steps(sem(f"{tag}_sa"), [f"sq{m}" for m in range(F)]), sem(f"{tag}_zero"))

        ffn_st = [ffn_steps("f0"), ffn_steps("f1")]

        HN = HEADS + KV_HEADS
        qkv_an, qkv_vn = [], []
        for j in range(HN):
            qkv_an += [f"g{j}"]
            if j - 1 >= HEADS:
                qkv_an += [f"khi{j - 1}"]
            qkv_an += [f"swap{j}_{q}" for q in range(4)]
            for jj in ([j - 1] if j else []):
                qkv_vn += [f"rec{jj}_{c}" for c in range(CHUNKS)] + [f"fin{jj}"]
                if jj >= HEADS:
                    qkv_vn += [f"dup{jj}", f"klo{jj}"]
            qkv_vn += [f"cos{j}", f"sin{j}", f"rope{j}"]
        qkv_an += ["v0", f"khi{HN - 1}", "v1", "v2"]
        qkv_vn += [f"rec{HN - 1}_{c}" for c in range(CHUNKS)] + [f"fin{HN - 1}", f"dup{HN - 1}", f"klo{HN - 1}"]
        qkv_a, qkv_v = Steps(sem("qkv_a"), qkv_an), Steps(sem("qkv_v"), qkv_vn)

        att_a = Steps(sem("att_a"), [f"{n}{u}" for u in range(HEADS) for n in ("e", "qh", "hi0_", "hi1_", "hi2_")], base=2)
        att_v = Steps(sem("att_v"), [f"{n}{u}" for u in range(HEADS) for n in ("mx", "neg", "ql", "sum", "rcp", "scale")],
                      base=7 + 6 * HEADS)

        end_a = Steps(sem("att_end_a"), [f"{n}{u}" for u in range(HEADS) for n in ("e", "hi0_", "hi1_", "hi2_")
                                         if n != "e" or u < HEADS - 1])
        end_v = Steps(sem("att_end_v"), [f"{n}{u}" for u in range(HEADS - 1) for n in ("mx", "neg", "sum", "rcp", "scale")])

        rows = [slice(c * CW, (c + 1) * CW) for c in range(CHUNKS)]

        def chunked(tile):
            return tile.rearrange("p (c w) -> p c w", c=CHUNKS)

        def over_f(tile):
            return tile.unsqueeze(1).broadcast_to([P, F, CW])

        def gain(layer, which, f):
            n = GAIN + (layer * 4 + which) * F + f
            return prm[:, n:n + 1]

        norms = [
            (A_T0, 0, None, 1, 2, None, (0, 0)),
            (A_T1, 3, 0, 1, 2, (0, 1), (0, 2)),
            (A_T2, 1, 0, 2, 3, (0, 3), (1, 0)),
            (A_T3, 0, 1, 2, 3, (1, 1), (1, 2)),
            (A_T4, 2, 1, None, None, (1, 3), None),
        ]
        ffns = [(U_FFN0, J_FFN0, 1, 2, 3, 0, 1), (U_FFN1, J_FFN1, 2, 3, 0, 1, 2)]
        outs = [(U_LRU_OUT, J_LRU_OUT, 3, 1, 2, 0, 3), (U_ATT_OUT, J_ATT_OUT, 0, 2, 3, 1, 0)]
        SP_BASE = {1: 0, 2: 1, 3: 2}

        block = ctx.enter_context(nc.Block())

        @block.sync
        def _(eng):
            eng.dma_start(prm[:, :], params).then_inc(loaded, 16)
            for c in range(CHUNKS):
                eng.dma_start(fr[0][:, :, rows[c]], h0[:, :, rows[c]]).then_inc(loaded, 16)

            def load(n, i=None):
                slot, turn = ring(n, WRING, i, WRING)
                wait(eng, w_ready[slot], turn)
                which = n if i is None else n + i * WRING
                eng.dma_start(raw[:, slot, :], weights[which, :, :]).then_inc(raw_full[slot], 16)

            for n in range(WRING):
                load(n)
            with eng.Fori(0, UNITS // WRING - 1) as i:
                for n in range(WRING):
                    load(n + WRING, i)
            for n in range(UNITS // WRING * WRING, UNITS):
                load(n)
            t_v = t_steps[4][0]
            for c in range(CHUNKS):
                eng.wait_ge(t_v.sem, t_v.after(f"h{c}_{F - 1}"))
                eng.dma_start(out[:, :, rows[c]], fr[norms[4][1]][:, :, rows[c]]).then_inc(out_done, 16)
            eng.wait_ge(out_done, 16 * CHUNKS)

        @block.gpsimd
        def _(eng):
            nc.gpsimd.memset(ones[:, :], 1.0).then_inc(const_ready, 1)
            nc.gpsimd.memset(eps[:, :], EPS).then_inc(const_ready, 1)
            nc.gpsimd.memset(ident[:, :], 0.0).then_inc(const_ready, 1)
            eng.wait_ge(const_ready, 3)
            nc.gpsimd.affine_select(out=ident[:, :], in_=ident[:, :], compare_op=ALU.not_equal, fill=1.0, base=0,
                                    pattern=[[-1, P]], channel_multiplier=1).then_inc(const_ready, 1)

            ahead = {(U_LRU + 2) % WRING: 1}

            def split(n, i=None):
                slot, turn = ring(n, WRING, i, WRING)
                first = isinstance(turn, int) and turn == 0
                wait(eng, raw_full[slot], 16 * (turn + 1))
                if not first:
                    wait(eng, w_free[slot], turn + ahead.get(slot, 0))
                eng.sem_inc(split_begun, 1)
                nc.gpsimd.tensor_scalar(whi[:, slot, :], raw[:, slot, :], 1.0, None, ALU.mult).then_inc(hi_done, 1)
                wait(eng, hi_done, n + 1 if i is None else n + i * WRING + 1)
                nc.gpsimd.tensor_tensor(wlo[:, slot, :], raw[:, slot, :], whi[:, slot, :].bitcast(F32),
                                        ALU.subtract).then_inc(w_ready[slot], 1)

            def units(a, b):
                turns = (b - a) // WRING
                if turns > 1:
                    with eng.Fori(0, turns) as i:
                        for n in range(WRING):
                            split(a + n, i)
                    a += turns * WRING
                for n in range(a, b):
                    split(n)

            def u_lo(t):
                v, a, g = t_steps[t]
                lo = rr[norms[t][4]]
                for c in range(CHUNKS):
                    eng.wait_ge(a.sem, a.after(f"hi{c}"))
                    g.did(f"lo{c}", nc.gpsimd.tensor_tensor(
                        lo[:, :, rows[c]], scaled[:, :, :], rr[norms[t][3]][:, :, rows[c]].bitcast(F32), ALU.subtract))

            at = 0
            for t, until in ((0, U_LRU + 3), (1, U_FFN0 + 2), (2, U_QKV + 1), (3, U_FFN1 + 2)):
                units(at, until)
                at = until
                u_lo(t)
            units(at, UNITS)

        @block.tensor
        def _(eng):
            held = [(U_LRU + 2) % WRING]

            def mm(out_, lhs, rhs, start, stop):
                ins = nc.tensor.matmul(out_, lhs, rhs, start=start, stop=stop)
                return ins

            def free_held(ins):
                if held:
                    ins.then_inc(w_free[held.pop(0)], 1)

            def job(n, i, per, parts, chunk_ready=None, unit=None, unit_per=0, width=CW, after_k=None):
                slot, turn = main(n, i, per)
                wait(eng, main_free[slot], turn)
                if unit is not None:
                    for u in unit:
                        s, t = ring(u, WRING, i, unit_per)
                        wait(eng, w_ready[s], t + 1)
                for c in range(CHUNKS):
                    if chunk_ready is not None:
                        chunk_ready(c)
                    todo = parts(c)
                    for k, (sh, sl, mh, ml) in enumerate(todo):
                        if after_k is not None:
                            after_k(c, k)
                        dst = slots[slot][0:sh.shape[1], c, 0:width]
                        last = k == len(todo) - 1
                        a = mm(dst, sh, mh, k == 0, False)
                        if k == 0:
                            free_held(a)
                        b = mm(dst, sh, ml, False, False)
                        d = mm(dst, sl, mh, False, last)
                d.then_inc(main_full[slot], 1)

            def from_u(u, hi, lo):
                s = u % WRING
                return lambda c: [(whi[:, s, k * P:(k + 1) * P], wlo[:, s, k * P:(k + 1) * P],
                                   rr[hi][:, k, rows[c]], rr[lo][:, k, rows[c]]) for k in range(F)]

            def release(*units):
                assert not held
                held.extend(u % WRING for u in units)

            def norm(t):
                base, h, m, hi, lo, g1, g0 = norms[t]
                v, a, g = t_steps[t]
                if m is not None:
                    s = out_st[t // 2][2] if t in (1, 3) else ffn_st[t // 2 - 1][2]
                    eng.wait_ge(s.sem, s.after(f"sum{F - 1}"))
                    for c in range(CHUNKS):
                        b, turn = aux(base + c)
                        wait(eng, aux_free[b], turn)
                        mm(banks[b][:, 0:CW], ones[:, :], sumsq[:, rows[c]], True, True).then_inc(aux_full[b], 1)
                    base += CHUNKS
                if hi is not None:
                    for c in range(CHUNKS):
                        b, turn = aux(base + c)
                        wait(eng, aux_free[b], turn)
                        eng.wait_ge(a.sem, a.after(f"sq{c}"))
                        for f in range(F):
                            ins = mm(banks[b][:, 0:CW], ones[:, :], squares[:, f, :], f == 0, f == F - 1)
                        ins.then_inc(aux_full[b], 1)

            def u_ready(t):
                g = t_steps[t][2]
                return lambda c: eng.wait_ge(g.sem, g.after(f"lo{c}"))

            eng.wait_ge(const_ready, 4)
            norm(0)
            with eng.Fori(0, F) as i:
                jx = lambda n, **k: job(J_LRU + n, i, 6, unit_per=3, **k)
                jx(0, parts=from_u(U_LRU, 1, 2), unit=[U_LRU], chunk_ready=u_ready(0))
                release(U_LRU)
                jx(1, parts=from_u(U_LRU + 1, 1, 2), unit=[U_LRU + 1])
                release(U_LRU + 1)
                s = (U_LRU + 2) % WRING
                eng.wait_ge(lru_v.sem, lru_v.after("xc_lo", i))
                for gate in range(4):
                    col = slice(gate * P, (gate + 1) * P)
                    jx(2 + gate, parts=lambda c: [(whi[:, s, col], wlo[:, s, col], xch[:, rows[c]], xcl[:, rows[c]])],
                       unit=[U_LRU + 2])
                release(U_LRU + 2)

            def mixer_out(layer):
                u0, j0, src, hi, lo, m, back = outs[layer]
                split_v = out_st[layer][0]
                for n in range(F):
                    ready = (lambda c, k: eng.wait_ge(split_v.sem, k + 1) if c == 0 else None) if n == 0 else None
                    job(j0 + n, None, 0, from_u(u0 + n, hi, lo), unit=[u0 + n], after_k=ready)
                    release(u0 + n)

            def ffn(layer, t):
                u0, j0, hi, lo, mid, acc, back = ffns[layer]
                v = ffn_st[layer][0]

                def up(n, u, i=None, chunk_ready=None):
                    job(j0 + n, i, 12, from_u(u0 + u, hi, lo), unit=[u0 + u], unit_per=6, chunk_ready=chunk_ready)
                    release(u0 + u)

                def down(n, u, i, first):
                    wait(eng, v.sem, v.after("lo_b", i) if i is not None else v.after("lo_b", FF // 2 - 1))
                    for f in range(F):
                        col = slice(f * P, (f + 1) * P)
                        job(j0 + n + f, i, 12, lambda c: [
                            (whi[:, (u0 + u + k) % WRING, col], wlo[:, (u0 + u + k) % WRING, col],
                             rr[mid][:, 2 * k, rows[c]], rr[mid][:, 2 * k + 1, rows[c]]) for k in range(2)],
                            unit=[u0 + u, u0 + u + 1], unit_per=6)
                    release(u0 + u, u0 + u + 1)

                for n in range(4):
                    up(n, n, None, u_ready(t) if n == 0 else None)
                with eng.Fori(0, FF // 2 - 1) as i:
                    up(4, 4, i)
                    up(5, 5, i)
                    down(6, 6, i, False)
                    up(14, 8, i)
                    up(15, 9, i)
                down(FFN_JOBS - F, FFN_UNITS - 2, None, True)

            mixer_out(0)
            norm(1)
            ffn(0, 1)
            norm(2)

            def head_sum(j):
                for c in range(CHUNKS):
                    b, turn = aux(A_QKV + j * CHUNKS + c)
                    wait(eng, aux_free[b], turn)
                    mm(banks[b][:, 0:CW], ones[:, :], hsq[:, rows[c]], True, True).then_inc(aux_full[b], 1)

            def head_squares_ready(j):
                s, t = main(J_QKV + j)
                eng.wait_ge(main_free[s], t + 1)

            for j in range(HN):
                job(J_QKV + j, None, 0, from_u(U_QKV + j, 2, 3), unit=[U_QKV + j], chunk_ready=u_ready(2) if j == 0 else None)
                release(U_QKV + j)
                if j:
                    head_squares_ready(j - 1)
                    head_sum(j - 1)
            for t in range(VJOBS):
                uv = [U_QKV + HN, U_QKV + HN + 1]

                def v_parts(c, t=t):
                    tok = slice((CHUNKS * t + c) * QW, (CHUNKS * t + c + 1) * QW)
                    parts = []
                    for k in range(F):
                        s = uv[k // 4] % WRING
                        col = slice((k % 4) * 256, (k % 4 + 1) * 256)
                        parts.append((rr[2][:, k, tok], rr[3][:, k, tok], whi[:, s, col], wlo[:, s, col]))
                    return parts

                job(J_QKV + HN + t, None, 0, v_parts, unit=uv, width=KV_HEADS * HEAD_DIM)
                if t == 0:
                    head_squares_ready(HN - 1)
                    head_sum(HN - 1)
            release(*uv)

            KH = lambda kv: (rr[1][:, kv, :], rr[1][:, 2 + kv, :])
            flat1 = rr[1][:, :, :].rearrange("p f t -> p (f t)")
            vhi = flat1[:, 4 * TOKENS:4 * TOKENS + QT * 256].rearrange("p (k d) -> p k d", k=QT)
            PT = [[rr[r][:, :, :].rearrange("p f t -> p (f t)")[:, kv * QT * GROUP * QW:(kv + 1) * QT * GROUP * QW]
                   .rearrange("p (k h q) -> p k h q", k=QT, h=GROUP) for r in (2, 3)] for kv in range(KV_HEADS)]

            def scores(u, i):
                wait(eng, att_v.sem, slice_ready(u, i))
                kh, kl = KH((u % HEADS) // GROUP)
                job(J_ATT + u, i, HEADS, lambda c: [(qsh[:, u % HEADS, :], qsl[:, u % HEADS, :], kh[:, rows[c]], kl[:, rows[c]])])

            def slice_ready(u, i):
                if u < HEADS:
                    return 1 if i is None else att_v.after(f"ql{u}", i) - len(att_v.names)
                return att_v.after(f"ql{u - HEADS}", i)

            def transposes(u, i):
                if u == 0:
                    wait(eng, att_v.sem, att_v.base + len(att_v.names) * i)
                elif isinstance(i, int):
                    wait(eng, end_v.sem, end_v.after(f"scale{u - 1}"))
                else:
                    wait(eng, att_v.sem, att_v.after(f"scale{u - 1}", i))
                for t in range(CHUNKS):
                    b, turn = aux(A_ATT + 3 * u + t + (u > 4), i, ATT_AUX)
                    wait(eng, aux_free[b], turn)
                    for k in range(3):
                        kt = 3 * t + k
                        ins = nc.tensor.transpose(banks[b][0:QW, k * QW:(k + 1) * QW],
                                                  prob[0:QW, u % 2, kt * QW:(kt + 1) * QW], ident[0:QW, 0:QW])
                    ins.then_inc(aux_full[b], 1)

            def values(kv, i):
                n = A_ATT + (15 if kv == 0 else 25)
                last = A_ATT + (11 if kv == 0 else 24)
                for d in (0, 1):
                    b, turn = aux(last - d, i, ATT_AUX)
                    wait(eng, aux_free[b], turn + 1)
                b, turn = aux(n, i, ATT_AUX)
                wait(eng, aux_free[b], turn)
                hi, lo = PT[kv]
                cols = slice(kv * HEAD_DIM, (kv + 1) * HEAD_DIM)
                for kt in range(QT):
                    dst = banks[b][:, 0:GROUP * QW]
                    mh = hi[0:QW, kt, :, :].rearrange("p h q -> p (h q)")
                    ml = lo[0:QW, kt, :, :].rearrange("p h q -> p (h q)")
                    mm(dst, vhi[0:QW, kt, cols], mh, kt == 0, False)
                    mm(dst, vhi[0:QW, kt, cols], ml, False, False)
                    ins = mm(dst, vlo[0:QW, kt, cols], mh, False, kt == QT - 1)
                ins.then_inc(aux_full[b], 1)

            def tile_steps(i, ahead):
                for u in range(HEADS):
                    if u + 2 < HEADS or ahead:
                        scores(u + 2, i)
                    transposes(u, i)
                    if u == 4:
                        values(0, i)
                values(1, i)

            eng.wait_ge(qkv_v.sem, qkv_v.after(f"klo{HN - 1}"))
            for u in range(2):
                eng.wait_ge(att_v.sem, 1)
                kh, kl = KH(0)
                job(J_ATT + u, None, 0, lambda c: [(qsh[:, u, :], qsl[:, u, :], kh[:, rows[c]], kl[:, rows[c]])])
            s, t = main(J_QKV + HN + VJOBS - 1)
            eng.wait_ge(main_free[s], t + 1)
            with eng.Fori(0, QT - 1) as i:
                tile_steps(i, True)
            tile_steps(QT - 1, False)

            mixer_out(1)
            norm(3)
            ffn(1, 3)
            norm(4)

        @block.scalar
        def _(eng):
            act = nc.scalar.activation

            def full(n, i=None, per=0):
                s, t = main(n, i, per)
                eng.wait_ge(main_full[s], t + 1)
                return s

            def norm(t):
                base, h, m, hi, lo, g1, g0 = norms[t]
                v, a, g = t_steps[t]

                def sqrt(n, c):
                    b, turn = aux(n)
                    eng.wait_ge(aux_full[b], turn + 1)
                    act(root[:, c, :], banks[b][:, 0:CW], ACT.Sqrt, bias=eps[:, 0:1], scale=1.0 / D_MODEL).then_inc(aux_free[b], 1)

                if m is not None:
                    for c in range(CHUNKS):
                        sqrt(base + c, c)
                    base += CHUNKS
                if hi is None:
                    return

                def sq(c):
                    if m is not None:
                        eng.wait_ge(v.sem, v.after(f"h{c}_{F - 1}"))
                    elif c == 0:
                        eng.wait_ge(loaded, 16 * (1 + CHUNKS))
                    if c:
                        b, turn = aux(base + c - 1)
                        eng.wait_ge(aux_full[b], turn + 1)
                    a.did(f"sq{c}", act(squares[:, :, :], fr[h][:, :, rows[c]], ACT.Square))

                def high(c):
                    eng.wait_ge(v.sem, v.after(f"u{c}_{F - 1}"))
                    a.did(f"hi{c}", act(rr[hi][:, :, rows[c]], scaled[:, :, :], ACT.Copy))

                sq(0)
                sqrt(base, 0)
                sq(1)
                high(0)
                sqrt(base + 1, 1)
                sq(2)
                high(1)
                sqrt(base + 2, 2)
                high(2)
                eng.dma_start(spill, fr[h][:, :, :]).then_inc(h_spilled, 16)
                return

            eng.wait_ge(sp_v.sem, 1)
            sp_a.did("exp", act(sp[:, 1, :], sp[:, 0, :], ACT.Exp, scale=-1.0))
            eng.wait_ge(const_ready, 4)
            norm(0)
            eng.wait_ge(h_spilled, 16)
            eng.wait_ge(sp_v.sem, sp_v.after("s22"))
            rt = fr[0]
            with eng.Fori(0, F) as i:
                v, a = lru_v, lru_a
                s = full(J_LRU, i, 6)
                act(chunked(xpad[:, CONV_LEFT:CONV_LEFT + TOKENS]), slots[s][:, :, 0:CW], ACT.Copy).then_inc(main_free[s], 1)
                _, t = main(J_LRU, i, 6)
                eng.wait_ge(main_free[s], t + 1)
                eng.wait_ge(v.sem, v.after("ix1", i) - len(lru_vn))
                a.did("tap0", act(xc[:, :], xpad[:, 0:TOKENS], ACT.Identity, bias=prm[:, bass.ds(i + CONVB, 1)],
                                  scale=prm[:, bass.ds(i + CONVW, 1)]))
                eng.wait_ge(v.sem, v.after("tap3", i))
                a.did("xc_hi", act(xch[:, :], xc[:, :], ACT.Copy))
                s = full(J_LRU + 1, i, 6)
                act(chunked(fr[3][:, i, :]), slots[s][:, :, 0:CW], ACT.Gelu_apprx_tanh).then_inc(main_free[s], 1)
                eng.wait_ge(v.sem, v.after("z", i) - len(lru_vn))
                for g in range(4):
                    s = full(J_LRU + 2 + g, i, 6)
                    act(chunked(rt[:, g, :]), slots[s][:, :, 0:CW], ACT.Sigmoid,
                        bias=prm[:, bass.ds(i + (GATEB + g * F), 1)]).then_inc(main_free[s], 1)
                for d in range(2):
                    s, t = main(J_LRU + 2 + 2 * d, i, 6)
                    eng.wait_ge(main_free[s], t + 1)
                    a.did(f"a{d}", act(rt[:, 4 + d, :], rt[:, 2 * d, :], ACT.Exp, scale=sp[:, 4, bass.ds(i + d * F, 1)]))
                for d in range(2):
                    eng.wait_ge(a.sem, a.after(f"a{d}", i))
                    a.did(f"t{d}", act(rt[:, 2 * d, :], rt[:, 2 * d, :], ACT.Tanh, scale=sp[:, 5, bass.ds(i + d * F, 1)]))
                for d in range(2):
                    a.did(f"sq{d}", act(rt[:, 6 + d, :], rt[:, 4 + d, :], ACT.Square))
                for d in range(2):
                    eng.wait_ge(v.sem, v.after(f"q{d}", i))
                    a.did(f"root{d}", act(rt[:, 6 + d, :], rt[:, 6 + d, :], ACT.Sqrt))

            def mixer_out(layer):
                u0, j0, src, hi, lo, m, back = outs[layer]
                sv, sa, v, a = out_st[layer]
                if layer == 0:
                    eng.wait_ge(lru_v.sem, lru_v.after("z", F - 1))
                else:
                    for n in (15, 25):
                        b, turn = aux(A_ATT + n + (QT - 1) * ATT_AUX)
                        eng.wait_ge(aux_free[b], turn + 1)
                with eng.Fori(0, F) as i:
                    sa.did("hi", act(rr[hi][:, i, :], fr[src][:, i, :], ACT.Copy))
                eng.wait_ge(sv.sem, F)
                eng.wait_ge(h_spilled, 16 * (1 + 2 * layer))
                eng.dma_start(fr[back][:, :, :], spill).then_inc(h_back, 16)
                for n in range(F):
                    s = full(j0 + n)
                    a.did(f"copy{n}", act(chunked(fr[m][:, n, :]), slots[s][:, :, 0:CW], ACT.Copy))
                    if n > 1:
                        eng.wait_ge(v.sem, v.after(f"sum{n - 1}"))
                    act(chunked(sqtile[:, :] if n else sumsq[:, :]), slots[s][:, :, 0:CW], ACT.Square).then_inc(main_free[s], 1)

            def ffn(layer):
                u0, j0, hi, lo, mid, acc, back = ffns[layer]
                v, a, sv, sa, zero = ffn_st[layer]

                def silu(n, i, u_before):
                    s = full(j0 + n, i, 12)
                    if u_before is not None:
                        sb, tb = main(j0 + u_before, i, 12)
                        wait(eng, main_free[sb], tb + 1)
                    act(chunked(fr[mid][:, 4, :]), slots[s][:, :, 0:CW], ACT.Silu).then_inc(main_free[s], 1)

                def high(x, n, i):
                    s, t = main(j0 + n, i, 12)
                    eng.wait_ge(main_free[s], t + 1)
                    a.did(f"hi_{x}", act(rr[mid][:, 2 * (x == "b"), :], fr[mid][:, 5, :], ACT.Copy))

                eng.wait_ge(h_spilled, 16 * (2 + 2 * layer))
                silu(0, None, None)
                high("a", 1, None)
                silu(2, None, 1)
                high("b", 3, None)
                with eng.Fori(0, FF // 2 - 1) as i:
                    silu(4, i, 3)
                    full(j0 + 13, i, 12)
                    high("a", 5, i)
                    silu(14, i, 5)
                    high("b", 15, i)
                eng.dma_start(fr[back][:, :, :], spill).then_inc(h_back, 16)
                for f in range(F):
                    s, t = main(j0 + FFN_JOBS - F + f)
                    eng.wait_ge(main_free[s], t + 1)
                    if f > 1:
                        eng.wait_ge(sv.sem, sv.after(f"sum{f - 1}"))
                    sa.did(f"sq{f}", act(sqtile[:, :] if f else sumsq[:, :], fr[acc][:, f, :], ACT.Square))

            mixer_out(0)
            norm(1)
            ffn(0)
            norm(2)

            eng.wait_ge(t_steps[2][2].sem, t_steps[2][2].after("lo2"))
            eng.dma_start(cossin[:, :, :], rope).then_inc(tables_in, 16)
            eng.wait_ge(h_spilled, 16 * 3)
            a, v = qkv_a, qkv_v
            kf = fr[1][:, :, :].rearrange("p f t -> p (f t)")[:, 4 * TOKENS + QT * 256:5 * TOKENS + QT * 256]
            flat1 = rr[1][:, :, :].rearrange("p f t -> p (f t)")
            vhi = flat1[:, 4 * TOKENS:4 * TOKENS + QT * 256].rearrange("p (k d) -> p k d", k=QT)

            def head_roots(j):
                for c in range(CHUNKS):
                    b, turn = aux(A_QKV + j * CHUNKS + c)
                    eng.wait_ge(aux_full[b], turn + 1)
                    if j:
                        eng.wait_ge(v.sem, v.after(f"rec{j - 1}_{c}"))
                    act(hroot[:, c, :], banks[b][:, 0:CW], ACT.Sqrt, bias=eps[:, 0:1], scale=1.0 / HEAD_DIM).then_inc(aux_free[b], 1)

            def k_high(j):
                eng.wait_ge(v.sem, v.after(f"dup{j}"))
                a.did(f"khi{j}", act(rr[1][:, j - HEADS, :], kf, ACT.Copy))

            def v_high(t):
                s = full(J_QKV + HN + t)
                a.did(f"v{t}", act(vhi[0:QW, 3 * t:3 * t + 3, :], slots[s][0:QW, :, 0:256], ACT.Copy))

            for j in range(HN):
                s = full(J_QKV + j)
                g = QGAIN if j < HEADS else KGAIN
                if j:
                    eng.wait_ge(v.sem, v.after(f"rope{j - 1}"))
                a.did(f"g{j}", act(chunked(hg[:, :]), slots[s][:, :, 0:CW], ACT.Identity, scale=prm[:, g:g + 1]))
                if j:
                    head_roots(j - 1)
                    if j - 1 >= HEADS:
                        k_high(j - 1)
                act(chunked(hsq[:, :]), slots[s][:, :, 0:CW], ACT.Square).then_inc(main_free[s], 1)
                eng.wait_ge(a.sem, a.after(f"g{j}"))
                for q in range(4):
                    a.did(f"swap{j}_{q}", act(hs[32 * q:32 * q + 32, :], hg[32 * (q ^ 1):32 * (q ^ 1) + 32, :], ACT.Copy))
            v_high(0)
            head_roots(HN - 1)
            k_high(HN - 1)
            v_high(1)
            v_high(2)

            a, v = att_a, att_v
            eng.wait_ge(qkv_v.sem, qkv_v.after(f"fin{HEADS - 1}"))
            eng.wait_ge(qkv_v.sem, qkv_v.after(f"klo{HN - 1}"))
            act(qsh[:, :, :], fr[0][:, :, 0:QW], ACT.Copy).then_inc(a.sem, 1)
            PT = [[rr[r][:, :, :].rearrange("p f t -> p (f t)")[:, kv * QT * GROUP * QW:(kv + 1) * QT * GROUP * QW]
                   .rearrange("p (k h q) -> p k h q", k=QT, h=GROUP) for r in (2, 3)] for kv in range(KV_HEADS)]

            def exps(u, i, neg, mark):
                s, _ = main(J_ATT + u, i, HEADS)
                b = u % 2
                eng.wait_ge(*neg)
                mark(act(chunked2(prob, b), slots[s][0:QW, 0:2, 0:CW], ACT.Exp, bias=stat[0:QW, b, 1:2],
                         accum_out=stat[0:QW, b, 2:3]))
                act(prob[0:QW, b, 2 * CW:REAL], slots[s][0:QW, 2, 0:CW - PAD], ACT.Exp, bias=stat[0:QW, b, 1:2],
                    accum_out=stat[0:QW, b, 3:4]).then_inc(main_free[s], 1)

            def chunked2(tile, b):
                return tile[0:QW, b, 0:2 * CW].rearrange("p (c w) -> p c w", c=2)

            def out_rows(kv, n, i):
                b, turn = aux(A_ATT + n, i, ATT_AUX)
                eng.wait_ge(aux_full[b], turn + 1)
                dst = fr[0][:, kv * GROUP:(kv + 1) * GROUP, bass.ds(i * QW, QW)]
                act(dst, banks[b][:, 0:GROUP * QW].rearrange("p (h q) -> p h q", h=GROUP), ACT.Copy).then_inc(aux_free[b], 1)

            def tile_steps(i, ahead):
                a, v, turn_ = (att_a, att_v, i) if ahead else (end_a, end_v, 0)
                for u in range(HEADS):
                    if u + 1 < HEADS or ahead:
                        exps(u + 1, i, (v.sem, v.after(f"neg{u}", turn_)), lambda x, u=u: a.did(f"e{u}", x))
                    if ahead:
                        a.did(f"qh{u}", act(qsh[:, u, :], fr[0][:, u, bass.ds(i * QW + QW, QW)], ACT.Copy))
                    if u == 5:
                        out_rows(0, 15, i)
                    for t in range(CHUNKS):
                        b, turn = aux(A_ATT + 3 * u + t + (u > 4), i, ATT_AUX)
                        eng.wait_ge(aux_full[b], turn + 1)
                        a.did(f"hi{t}_{u}", act(PT[u // GROUP][0][0:QW, 3 * t:3 * t + 3, u % GROUP, :],
                                                banks[b][0:QW, 0:CW].rearrange("p (k q) -> p k q", k=3), ACT.Copy))
                out_rows(1, 25, i)

            exps(0, None, (v.sem, len(v.names) + 4), lambda x: x.then_inc(a.sem, 1))
            with eng.Fori(0, QT - 1) as i:
                tile_steps(i, True)
            tile_steps(QT - 1, False)

            mixer_out(1)
            norm(3)
            ffn(1)
            norm(4)

        @block.vector
        def _(eng):
            vec = nc.vector

            def full(n, i=None, per=0):
                s, t = main(n, i, per)
                eng.wait_ge(main_full[s], t + 1)
                return s

            count = [0]

            def link(ins):
                sp_v.did(f"s{count[0]}", ins)
                count[0] += 1
                eng.wait_ge(sp_v.sem, count[0])

            eng.wait_ge(loaded, 16 * (1 + CHUNKS))
            lam = prm[:, LAM:LAM + 2 * F]
            link(vec.scalar_tensor_tensor(out=sp[:, 0, :], in0=lam, scalar=-1.0, in1=lam, op0=ALU.mult, op1=ALU.max))
            eng.wait_ge(sp_a.sem, 1)
            link(vec.tensor_scalar(sp[:, 2, :], sp[:, 1, :], 2.0, None, ALU.add))
            link(vec.reciprocal(sp[:, 3, :], sp[:, 2, :]))
            link(vec.tensor_tensor(sp[:, 0, :], sp[:, 1, :], sp[:, 3, :], ALU.mult))
            link(vec.tensor_tensor(sp[:, 1, :], sp[:, 0, :], sp[:, 0, :], ALU.mult))
            link(vec.tensor_scalar(sp[:, 2, :], sp[:, 1, :], 1.0 / 15, 1.0 / 13, ALU.mult, ALU.add))
            for d in (11, 9, 7, 5, 3, 1):
                link(vec.tensor_tensor(sp[:, 3, :], sp[:, 2, :], sp[:, 1, :], ALU.mult))
                link(vec.tensor_scalar(sp[:, 2, :], sp[:, 3, :], 1.0 / d, None, ALU.add))
            link(vec.tensor_tensor(sp[:, 3, :], sp[:, 2, :], sp[:, 0, :], ALU.mult))
            link(vec.tensor_scalar(sp[:, 0, :], lam, -1.0, 0.0, ALU.mult, ALU.max))
            link(vec.scalar_tensor_tensor(out=sp[:, 2, :], in0=sp[:, 3, :], scalar=2.0, in1=sp[:, 0, :],
                                          op0=ALU.mult, op1=ALU.add))
            link(vec.tensor_scalar(sp[:, 4, :], sp[:, 2, :], -LRU_C, None, ALU.mult))
            link(vec.tensor_scalar(sp[:, 5, :], sp[:, 2, :], LRU_C, None, ALU.mult))

            def norm(t):
                base, h, m, hi, lo, g1, g0 = norms[t]
                v, a, g = t_steps[t]

                def recip(n, c, name):
                    b, turn = aux(n)
                    eng.wait_ge(aux_free[b], turn + 1)
                    v.did(name, vec.reciprocal(rstd[:, c, :], root[:, c, :]))
                    eng.wait_ge(v.sem, v.after(name))

                def update(c):
                    if m is None:
                        return
                    recip(base + c, c, f"rm{c}")
                    if c == 0:
                        eng.wait_ge(h_back, 16 * t)
                    v.did(f"mr{c}", vec.tensor_tensor(fr[m][:, :, rows[c]], fr[m][:, :, rows[c]], over_f(rstd[:, c, :]), ALU.mult))
                    eng.wait_ge(v.sem, v.after(f"mr{c}"))
                    for f in range(F):
                        v.did(f"h{c}_{f}", vec.scalar_tensor_tensor(
                            out=fr[h][:, f, rows[c]], in0=fr[m][:, f, rows[c]], scalar=gain(*g1, f),
                            in1=fr[h][:, f, rows[c]], op0=ALU.mult, op1=ALU.add))

                def normed(c):
                    if hi is None:
                        return
                    n = base + (CHUNKS if m is not None else 0) + c
                    recip(n, c, f"rh{c}")
                    if c:
                        eng.wait_ge(g.sem, g.after(f"lo{c - 1}"))
                    for f in range(F):
                        v.did(f"u{c}_{f}", vec.scalar_tensor_tensor(
                            out=scaled[:, f, :], in0=fr[h][:, f, rows[c]], scalar=gain(*g0, f),
                            in1=rstd[:, c, :], op0=ALU.mult, op1=ALU.mult))

                update(0)
                update(1)
                normed(0)
                update(2)
                normed(1)
                normed(2)

            norm(0)
            eng.wait_ge(t_steps[0][2].sem, t_steps[0][2].after("lo2"))
            rt = fr[0]
            vec.memset(xpad[:, 0:CONV_LEFT], 0.0)
            vec.memset(xpad[:, CONV_LEFT + TOKENS:], 0.0).then_inc(lru_v.sem, len(lru_vn))
            with eng.Fori(0, F) as i:
                v, a = lru_v, lru_a
                eng.wait_ge(a.sem, a.after("tap0", i))
                for k in range(1, CONV_W):
                    if k > 1:
                        eng.wait_ge(v.sem, v.after(f"tap{k - 1}", i))
                    v.did(f"tap{k}", vec.scalar_tensor_tensor(
                        out=xc[:, :], in0=xpad[:, k:k + TOKENS], scalar=prm[:, bass.ds(i + (CONVW + k * F), 1)],
                        in1=xc[:, :], op0=ALU.mult, op1=ALU.add))
                eng.wait_ge(a.sem, a.after("xc_hi", i))
                v.did("xc_lo", vec.tensor_tensor(xcl[:, :], xc[:, :], xch[:, :].bitcast(F32), ALU.subtract))
                for d in range(2):
                    s, t = main(J_LRU + 3 + 2 * d, i, 6)
                    eng.wait_ge(main_free[s], t + 1)
                    v.did(f"ix{d}", vec.tensor_tensor(rt[:, 1 + 2 * d, :], rt[:, 1 + 2 * d, :], xc[:, :], ALU.mult))
                for d in range(2):
                    eng.wait_ge(a.sem, a.after(f"sq{d}", i))
                    v.did(f"q{d}", vec.scalar_tensor_tensor(out=rt[:, 6 + d, :], in0=rt[:, 6 + d, :], scalar=1.0,
                                                            in1=rt[:, 2 * d, :], op0=ALU.add, op1=ALU.mult))
                for d in range(2):
                    eng.wait_ge(a.sem, a.after(f"root{d}", i))
                    v.did(f"b{d}", vec.tensor_tensor(rt[:, 6 + d, :], rt[:, 6 + d, :], rt[:, 1 + 2 * d, :], ALU.mult))
                    eng.wait_ge(v.sem, v.after(f"b{d}", i))
                    way = (lambda x: x[:, 0:REAL]) if d == 0 else (lambda x: x[:, REAL - 1::-1])
                    v.did(f"scan{d}", vec.tensor_tensor_scan(way(rt[:, 2 * d, :]), way(rt[:, 4 + d, :]), way(rt[:, 6 + d, :]),
                                                             0.0, ALU.mult, ALU.add))
                eng.wait_ge(v.sem, v.after("scan1", i))
                v.did("rec", vec.tensor_tensor(rt[:, 0, :], rt[:, 0, :], rt[:, 2, :], ALU.add))
                eng.wait_ge(v.sem, v.after("rec", i))
                v.did("z", vec.tensor_tensor(fr[3][:, i, :], fr[3][:, i, :], rt[:, 0, :], ALU.mult))

            def mixer_out(layer):
                u0, j0, src, hi, lo, m, back = outs[layer]
                sv, sa, v, a = out_st[layer]
                with eng.Fori(0, F) as i:
                    eng.wait_ge(sa.sem, sa.after("hi", i))
                    sv.did("lo", vec.tensor_tensor(rr[lo][:, i, :], fr[src][:, i, :], rr[hi][:, i, :].bitcast(F32), ALU.subtract))
                for n in range(1, F):
                    s, t = main(j0 + n)
                    eng.wait_ge(main_free[s], t + 1)
                    if n > 1:
                        eng.wait_ge(v.sem, v.after(f"sum{n - 1}"))
                    v.did(f"sum{n}", vec.tensor_tensor(sumsq[:, :], sumsq[:, :], sqtile[:, :], ALU.add))

            def ffn(layer):
                u0, j0, hi, lo, mid, acc, back = ffns[layer]
                v, a, sv, sa, zero = ffn_st[layer]
                vec.memset(fr[acc][:, :, :], 0.0).then_inc(zero, 1)

                def mult(n, i, split=None):
                    if split is not None:
                        eng.wait_ge(v.sem, v.after(*split))
                    s, t = main(j0 + n - 1, i, 12)
                    eng.wait_ge(main_free[s], t + 1)
                    s = full(j0 + n, i, 12)
                    vec.tensor_tensor(chunked(fr[mid][:, 5, :]), slots[s][:, :, 0:CW], chunked(fr[mid][:, 4, :]),
                                      ALU.mult).then_inc(main_free[s], 1)

                def low(x, turn):
                    eng.wait_ge(a.sem, a.after(f"hi_{x}", turn))
                    row = 2 * (x == "b")
                    v.did(f"lo_{x}", vec.tensor_tensor(rr[mid][:, row + 1, :], fr[mid][:, 5, :],
                                                       rr[mid][:, row, :].bitcast(F32), ALU.subtract))

                def add(n, f, i):
                    s = full(j0 + n, i, 12)
                    vec.tensor_tensor(chunked(fr[acc][:, f, :]), slots[s][:, :, 0:CW], chunked(fr[acc][:, f, :]),
                                      ALU.add).then_inc(main_free[s], 1)

                mult(1, None)
                low("a", 0)
                eng.wait_ge(zero, 1)
                mult(3, None, ("lo_a", 0))
                low("b", 0)
                with eng.Fori(0, FF // 2 - 1) as i:
                    mult(5, i, ("lo_b", i))
                    for f in range(F):
                        add(6 + f, f, i)
                    low("a", i + 1)
                    mult(15, i, ("lo_a", i + 1))
                    low("b", i + 1)

                def square_sum(f):
                    eng.wait_ge(sa.sem, sa.after(f"sq{f}"))
                    if f > 1:
                        eng.wait_ge(sv.sem, sv.after(f"sum{f - 1}"))
                    sv.did(f"sum{f}", vec.tensor_tensor(sumsq[:, :], sumsq[:, :], sqtile[:, :], ALU.add))

                for f in range(F):
                    add(FFN_JOBS - F + f, f, None)
                    if f > 1:
                        square_sum(f - 1)
                square_sum(F - 1)

            mixer_out(0)
            norm(1)
            ffn(0)
            norm(2)

            a, v = qkv_a, qkv_v
            eng.wait_ge(tables_in, 16)
            eng.wait_ge(h_spilled, 16 * 3)
            flat1 = rr[1][:, :, :].rearrange("p f t -> p (f t)")
            vhi = flat1[:, 4 * TOKENS:4 * TOKENS + QT * 256].rearrange("p (k d) -> p k d", k=QT)
            kf = fr[1][:, :, :].rearrange("p f t -> p (f t)")[:, 4 * TOKENS + QT * 256:5 * TOKENS + QT * 256]

            def head_row(j):
                return fr[0][:, j, :] if j < HEADS else kf

            def head_norm(j):
                for c in range(CHUNKS):
                    b, turn = aux(A_QKV + j * CHUNKS + c)
                    eng.wait_ge(aux_free[b], turn + 1)
                    v.did(f"rec{j}_{c}", vec.reciprocal(hrstd[:, c, :], hroot[:, c, :]))
                eng.wait_ge(v.sem, v.after(f"rec{j}_{CHUNKS - 1}"))
                scale = HEAD_DIM ** -0.5 if j < HEADS else 1.0
                row = head_row(j)
                v.did(f"fin{j}", vec.scalar_tensor_tensor(out=chunked(row), in0=chunked(row), scalar=scale, in1=hrstd[:, :, :],
                                                          op0=ALU.mult, op1=ALU.mult))
                if j >= HEADS:
                    eng.wait_ge(v.sem, v.after(f"fin{j}"))
                    v.did(f"dup{j}", vec.tensor_copy(kf[:, REAL:TOKENS], kf[:, 0:PAD]))
                    eng.wait_ge(a.sem, a.after(f"khi{j}"))
                    v.did(f"klo{j}", vec.tensor_tensor(rr[1][:, 2 + j - HEADS, :], kf, rr[1][:, j - HEADS, :].bitcast(F32),
                                                       ALU.subtract))

            def v_low(t):
                s = full(J_QKV + HN + t)
                eng.wait_ge(a.sem, a.after(f"v{t}"))
                vec.tensor_tensor(vlo[0:QW, 3 * t:3 * t + 3, :], slots[s][0:QW, :, 0:256],
                                  vhi[0:QW, 3 * t:3 * t + 3, :].bitcast(F32), ALU.subtract).then_inc(main_free[s], 1)

            for j in range(HN):
                if j:
                    head_norm(j - 1)
                eng.wait_ge(a.sem, a.after(f"swap{j}_3"))
                v.did(f"cos{j}", vec.tensor_tensor(hg[:, :], hg[:, :], cossin[:, 0, :], ALU.mult))
                v.did(f"sin{j}", vec.tensor_tensor(hs[:, :], hs[:, :], cossin[:, 1, :], ALU.mult))
                eng.wait_ge(v.sem, v.after(f"sin{j}"))
                v.did(f"rope{j}", vec.tensor_tensor(head_row(j), hg[:, :], hs[:, :], ALU.add))
            v_low(0)
            head_norm(HN - 1)
            v_low(1)
            v_low(2)

            a, v = att_a, att_v
            PT = [[rr[r][:, :, :].rearrange("p f t -> p (f t)")[:, kv * QT * GROUP * QW:(kv + 1) * QT * GROUP * QW]
                   .rearrange("p (k h q) -> p k h q", k=QT, h=GROUP) for r in (2, 3)] for kv in range(KV_HEADS)]
            eng.wait_ge(a.sem, 1)
            vec.tensor_tensor(qsl[:, :, :], fr[0][:, :, 0:QW], qsh[:, :, :].bitcast(F32), ALU.subtract).then_inc(v.sem, 1)
            vec.memset(prob[:, :, REAL:TOKENS], 0.0).then_inc(v.sem, 1 + len(v.names))

            def row_max(u, i, mark1, wait1, mark2, sem=v.sem):
                s = full(J_ATT + u, i, HEADS)
                b = u % 2
                mark1(vec.tensor_reduce(stat[0:QW, b, 0:1], slots[s][0:QW, :, 0:CW], mybir.AxisListType.XY, ALU.max))
                eng.wait_ge(sem, wait1)
                mark2(vec.tensor_scalar(stat[0:QW, b, 1:2], stat[0:QW, b, 0:1], -1.0, None, ALU.mult))

            def normalise(u, i, marks, waits, sem=v.sem):
                s, t = main(J_ATT + u, i, HEADS)
                b = u % 2
                eng.wait_ge(main_free[s], t + 1)
                marks[0](vec.tensor_tensor(stat[0:QW, b, 4:5], stat[0:QW, b, 2:3], stat[0:QW, b, 3:4], ALU.add))
                eng.wait_ge(sem, waits[0])
                marks[1](vec.reciprocal(stat[0:QW, b, 5:6], stat[0:QW, b, 4:5]))
                eng.wait_ge(sem, waits[1])
                marks[2](vec.tensor_scalar(prob[0:QW, b, 0:REAL], prob[0:QW, b, 0:REAL], stat[0:QW, b, 5:6], None, ALU.mult))

            inc = lambda x: x.then_inc(v.sem, 1)
            ahead_of = len(v.names)
            row_max(0, None, inc, ahead_of + 3, inc)
            normalise(0, None, (inc, inc, inc), (ahead_of + 5, ahead_of + 6))

            def tile_steps(i, ahead):
                a, v, turn_ = (att_a, att_v, i) if ahead else (end_a, end_v, 0)
                for u in range(HEADS):
                    more = u + 1 < HEADS or ahead
                    if more:
                        row_max(u + 1, i, lambda x: v.did(f"mx{u}", x), v.after(f"mx{u}", turn_),
                                lambda x: v.did(f"neg{u}", x), v.sem)
                    if ahead:
                        eng.wait_ge(a.sem, a.after(f"qh{u}", i))
                        v.did(f"ql{u}", vec.tensor_tensor(qsl[:, u, :], fr[0][:, u, bass.ds(i * QW + QW, QW)],
                                                          qsh[:, u, :].bitcast(F32), ALU.subtract))
                    if more:
                        normalise(u + 1, i, [lambda x, n=n: v.did(f"{n}{u}", x) for n in ("sum", "rcp", "scale")],
                                  (v.after(f"sum{u}", turn_), v.after(f"rcp{u}", turn_)), v.sem)
                    for t in range(CHUNKS):
                        b, turn = aux(A_ATT + 3 * u + t + (u > 4), i, ATT_AUX)
                        eng.wait_ge(a.sem, a.after(f"hi{t}_{u}", turn_))
                        src = banks[b][0:QW, 0:CW].rearrange("p (k q) -> p k q", k=3)
                        vec.tensor_tensor(PT[u // GROUP][1][0:QW, 3 * t:3 * t + 3, u % GROUP, :], src,
                                          PT[u // GROUP][0][0:QW, 3 * t:3 * t + 3, u % GROUP, :].bitcast(F32),
                                          ALU.subtract).then_inc(aux_free[b], 1)

            with eng.Fori(0, QT - 1) as i:
                tile_steps(i, True)
            tile_steps(QT - 1, False)

            mixer_out(1)
            norm(3)
            ffn(1)
            norm(4)


def unit_of(w, c0, cols=P):
    k = w.shape[0] // P
    return w[:, c0:c0 + cols].reshape(k, P, cols).transpose(1, 0, 2).reshape(P, k * cols)


def lay_out_weights(lru_w_in, lru_gate_w, lru_w_out, attn_w_qkv, attn_w_out, ffn_w_in, ffn_w_out):
    units = []
    for n in range(F):
        units.append(unit_of(lru_w_in[0], D_MODEL + n * P))
        units.append(unit_of(lru_w_in[0], n * P))
        g = lru_gate_w[0][:, :, n].reshape(4, P, P).transpose(1, 0, 2).reshape(P, 4 * P)
        units.append(np.concatenate([g, g], axis=1))
    units += [unit_of(lru_w_out[0], n * P) for n in range(F)]

    def ffn(layer):
        w_in, w_out = ffn_w_in[layer], ffn_w_out[layer]
        up = lambda r: [unit_of(w_in, r * P), unit_of(w_in, D_FF + r * P)]
        down = lambda r: [w_out[r * P:(r + 1) * P, :]]
        got = up(0) + up(1)
        for g in range(1, FF // 2):
            got += up(2 * g) + down(2 * g - 2) + down(2 * g - 1) + up(2 * g + 1)
        return got + down(FF - 2) + down(FF - 1)

    units += ffn(0)
    units += [unit_of(attn_w_qkv[0], n * P) for n in range(HEADS + KV_HEADS)]
    v0 = (HEADS + KV_HEADS) * P
    for half in range(2):
        units.append(unit_of(attn_w_qkv[0][half * 512:(half + 1) * 512], v0, KV_HEADS * P))
    units += [unit_of(attn_w_out[0], n * P) for n in range(F)]
    units += ffn(1)
    assert len(units) == UNITS
    return np.ascontiguousarray(np.stack(units))


def rope_tables():
    grid_w, pairs = 64, HEAD_DIM // 4
    inv = (np.float32(10000.0) ** (-np.arange(0, 2 * pairs, 2, dtype=np.float32) / np.float32(2 * pairs))).astype(np.float32)
    ang = np.zeros((TOKENS, 2, pairs), np.float32)
    t = np.arange(SEQ)
    ang[N_META:REAL, 0] = (t // grid_w).astype(np.float32)[:, None] * inv
    ang[N_META:REAL, 1] = (t % grid_w).astype(np.float32)[:, None] * inv
    cos, sin = np.cos(ang), np.sin(ang)
    tab = np.zeros((P, 2, TOKENS), np.float32)
    for axis in range(2):
        for half in range(2):
            at = axis * 64 + half * 32
            tab[at:at + 32, 0] = cos[:, axis].T
            tab[at:at + 32, 1] = (sin[:, axis].T if half else -sin[:, axis].T)
    return tab


def kernel(**inputs):
    import concourse.bacc as _bacc
    from concourse.bass_utils import run_bass_kernel_spmd as _run

    a = {k: np.asarray(v) for k, v in inputs.items()}
    tokens = np.concatenate([a["meta_tokens"], a["x"][0], np.zeros((PAD, D_MODEL), np.float32)], axis=0)
    h0 = np.ascontiguousarray(tokens.reshape(TOKENS, F, P).transpose(2, 1, 0))
    cols = [a["norm_gains"].reshape(8 * F, P), a["lru_conv_w"].reshape(CONV_W * F, P), a["lru_conv_b"].reshape(F, P),
            a["lru_gate_b"].reshape(4 * F, P), a["lru_lambda"].reshape(2 * F, P), a["attn_q_gain"].reshape(1, P),
            a["attn_k_gain"].reshape(1, P)]
    params = np.ascontiguousarray(np.concatenate(cols, axis=0).T)
    weights = lay_out_weights(*(a[n] for n in ("lru_w_in", "lru_gate_w", "lru_w_out", "attn_w_qkv", "attn_w_out",
                                               "ffn_w_in", "ffn_w_out")))
    arrays = {"h0_dram": h0, "params_dram": params, "rope_dram": rope_tables(), "weights_dram": weights}
    nc = _bacc.Bacc("TRN2", target_bir_lowering=False, num_devices=1)
    aps = [nc.dram_tensor(n, x.shape, F32, kind="ExternalInput").ap() for n, x in arrays.items()]
    out = nc.dram_tensor("out_dram", (P, F, TOKENS), F32, kind="ExternalOutput").ap()
    spill = nc.dram_tensor("spill_dram", (P, F, TOKENS), F32, kind="Internal").ap()
    trunk(nc, *aps, out, spill)
    r = _run(nc, [arrays], core_ids=[0])
    got = np.asarray(r.results[0]["out_dram"])
    return np.ascontiguousarray(got.transpose(2, 1, 0).reshape(TOKENS, D_MODEL)[N_META:REAL])[None]
```

```python
from contextlib import ExitStack, contextmanager

import numpy as np

import concourse.bass as bass
from concourse import mybir

ALU = mybir.AluOpType
ACT = mybir.ActivationFunctionType
AX_X = mybir.AxisListType.X
F32 = mybir.dt.float32
F32R = mybir.dt.float32r

P = 128
D_MODEL = 1024
F = D_MODEL // P
N_META, SEQ = 16, 1024
REAL = N_META + SEQ
CHUNKS = 3
CW = 348
TOKENS = CHUNKS * CW
PAD = TOKENS - REAL
EPS = 1e-6
D_FF = 2816
FF = D_FF // P
LRU_C = 8.0
CONV_W, CONV_LEFT = 4, 2
HEADS, KV_HEADS = 8, 2
GROUP = HEADS // KV_HEADS
HEAD_DIM = 128
QT = 9
QW = TOKENS // QT
UNIT = 1024
WRING = 3

GAIN = 0
CONVW = GAIN + 2 * 4 * F
CONVB = CONVW + CONV_W * F
GATEB = CONVB + F
LAM = GATEB + 4 * F
QGAIN = LAM + 2 * F
KGAIN = QGAIN + 1
PARAMS = KGAIN + 1

U_LRU = 0
U_LRU_OUT = U_LRU + 3 * F
U_FFN0 = U_LRU_OUT + F
FFN_UNITS = 3 * FF
U_QKV = U_FFN0 + FFN_UNITS
U_ATT_OUT = U_QKV + HEADS + 2 * KV_HEADS
U_FFN1 = U_ATT_OUT + F
UNITS = U_FFN1 + FFN_UNITS

OUT_ROWS = F - 2
LAST_ROWS = ((0, 3), (3, 6), (6, F))
FFN_JOBS = 2 * FF + (FF // 2 - 1) * F + CHUNKS * len(LAST_ROWS)
LAST_DOWN = FFN_JOBS - CHUNKS * len(LAST_ROWS)
VJOBS = QT // 3
J_LRU = 0
J_LRU_OUT = J_LRU + 6 * F
J_FFN0 = J_LRU_OUT + OUT_ROWS + CHUNKS
J_QKV = J_FFN0 + FFN_JOBS
J_ATT = J_QKV + HEADS + KV_HEADS + VJOBS
J_ATT_OUT = J_ATT + QT * HEADS
J_FFN1 = J_ATT_OUT + OUT_ROWS + CHUNKS

HN = HEADS + KV_HEADS
TURNED = HEADS * CHUNKS + KV_HEADS
A_NORM = [(0, 0), (CHUNKS, CHUNKS), (3 * CHUNKS, 3 * CHUNKS)]
A_QKV = (5 * CHUNKS, 5 * CHUNKS)
BEFORE = (A_QKV[0] + HN, A_QKV[1] + HN * CHUNKS)
A_NORM.append((BEFORE[0] + QT * TURNED, BEFORE[1] + QT * KV_HEADS))
A_NORM.append((A_NORM[3][0] + 2 * CHUNKS, A_NORM[3][1] + 2 * CHUNKS))


def ring(n, size, i=None, per=0):
    assert per % size == 0
    return n % size, n // size + (0 if i is None else i * (per // size))


def main(n, i=None, per=0):
    return ring(n, 2, i, per)


def norm_turn(bank, t, of_m, c):
    return A_NORM[t][bank] + (0 if of_m or t == 0 else CHUNKS) + c


def turned(k, i):
    skipped = not (isinstance(i, int) and i == 0 and k < SUMS_AFTER[1])
    return BEFORE[0] + k + TURNED * i - skipped


def summed(kv, i):
    return BEFORE[1] + kv + KV_HEADS * i


def wait(eng, sem, value):
    if not isinstance(value, int) or value > 0:
        eng.wait_ge(sem, value)


def turned_unit(u, t):
    return CHUNKS * u + t + (u > 1) + (u > 5)


SUMS_AFTER = {1: CHUNKS * 2, 5: CHUNKS * 6 + 1}
VALUES_AT = {0: ([], [], [0, 1]), 1: ([], [2], [3]), 2: ([4], [5], []), 3: ([6], [7], [8])}


class Steps:

    def __init__(self, sem, names, base=0):
        self.sem, self.names, self.base, self.at = sem, list(names), base, 0

    def after(self, name, i=0):
        return self.base + self.names.index(name) + 1 + len(self.names) * i

    def did(self, name, instruction):
        assert self.names[self.at % len(self.names)] == name, (name, self.names[self.at % len(self.names)])
        self.at += 1
        instruction.then_inc(self.sem, 1)


def trunk(nc, h0, params, rope, weights, out, spill):
    with ExitStack() as ctx:
        def sem(name):
            return ctx.enter_context(nc.semaphore(name))

        def keep(name, shape, dt):
            return ctx.enter_context(nc.sbuf_tensor(name, shape, dt))

        @contextmanager
        def overlay():
            with ExitStack() as own:
                yield lambda name, shape, dt: own.enter_context(nc.sbuf_tensor(name, shape, dt))

        prm = keep("prm", [P, PARAMS], F32)
        ones = keep("ones", [P, P], F32)
        ident = keep("ident", [P, P], F32)
        eps = keep("eps", [P, 1], F32)
        sp = keep("softplus", [P, 6, 2 * F], F32)
        stat = keep("stat", [P, 2, 8], F32)
        root_t = keep("root_t", [P, 2, QT], F32)
        rstd_t = keep("rstd_t", [P, 2, QT], F32)
        hroot_t = keep("hroot_t", [P, QT], F32)
        hrstd_t = keep("hrstd_t", [P, QT], F32)
        rsum = keep("rsum", [P, HEADS, 1], F32)
        raw = keep("raw", [P, WRING, UNIT], F32)
        whi = keep("whi", [P, WRING, UNIT], F32R)
        wlo = keep("wlo", [P, WRING, UNIT], F32R)

        fr, rr = [], []
        for n in range(4):
            with overlay() as sb:
                fr.append(sb(f"region{n}", [P, F, TOKENS], F32))
            rr.append(keep(f"region{n}r", [P, F, TOKENS], F32R))

        with ExitStack() as att:
            vlo = att.enter_context(nc.sbuf_tensor("vlo", [P, QT, KV_HEADS * HEAD_DIM], F32R))
            with overlay() as sb0:
                rstd = sb0("rstd", [P, CHUNKS, CW], F32)
                with overlay() as sb:
                    squares = sb("squares", [P, F, CW], F32)
                    rstd_m = sb("rstd_m", [P, CHUNKS, CW], F32)
                    sumsq = sb("sumsq", [P, TOKENS], F32)
                    sqtile = sb("sqtile", [P, TOKENS], F32)
                with overlay() as sb:
                    xpad = sb("xpad", [P, TOKENS + CONV_W - 1], F32)
                    xc = sb("xc", [P, TOKENS], F32)
                    xch = sb("xch", [P, TOKENS], F32R)
                    xcl = sb("xcl", [P, TOKENS], F32R)
                with overlay() as sb:
                    cossin = sb("cossin", [P, 2, TOKENS], F32)
                    hraw = sb("hraw", [P, TOKENS], F32)
                    hg = sb("hg", [P, TOKENS], F32)
                    hs = sb("hs", [P, TOKENS], F32)
                    hsq = sb("hsq", [P, TOKENS], F32)
            with overlay() as sb:
                prob = sb("prob", [P, 2, TOKENS], F32)
                turn_f = sb("turn_f", [P, 2, CHUNKS, CW], F32)
                recips = sb("recips", [P, GROUP * QW], F32)
                qsh = sb("qsh", [P, HEADS, QW], F32R)
                qsl = sb("qsl", [P, HEADS, QW], F32R)

        slots = [ctx.enter_context(nc.psum_tensor(f"slot{s}", [P, CHUNKS, 512], F32)) for s in range(2)]
        banks = [ctx.enter_context(nc.psum_tensor(f"bank{s}", [P, 512], F32)) for s in range(2)]

        main_full = [sem(f"main_full{s}") for s in range(2)]
        main_free = [sem(f"main_free{s}") for s in range(2)]
        aux_full = [sem(f"aux_full{s}") for s in range(2)]
        aux_free = [sem(f"aux_free{s}") for s in range(2)]
        raw_full = [sem(f"raw_full{s}") for s in range(WRING)]
        split_begun, hi_done = sem("split_begun"), sem("hi_done")
        w_ready = [sem(f"w_ready{s}") for s in range(WRING)]
        w_free = [sem(f"w_free{s}") for s in range(WRING)]
        params_in = sem("params_in")
        h_in = [sem(f"h_in{c}") for c in range(CHUNKS)]
        tables_in = sem("tables_in")
        const_ready = sem("const_ready")
        h_spilled, h_back, out_done = sem("h_spilled"), sem("h_back"), sem("out_done")

        sp_v = Steps(sem("sp_v"), [f"s{n}" for n in range(23)])
        sp_a = Steps(sem("sp_a"), ["exp"])

        recip_m, recip_h = sem("recip_m"), sem("recip_h")
        scaled_v, scaled_g = sem("scaled_v"), sem("scaled_g")
        h_new, h_squared = sem("h_new"), sem("h_squared")
        u_hi, u_lo = sem("u_hi"), sem("u_lo")
        rows_summed, m_squared = sem("rows_summed"), sem("m_squared")
        m_folded, m_folded_v, h_folded = sem("m_folded"), sem("m_folded_v"), sem("h_folded")
        zero = sem("acc_zero")

        def by_chunk(t, c):
            return CHUNKS * t + c + 1

        def by_row(t, c, f):
            return (CHUNKS * t + c) * F + f + 1

        lru_cv = Steps(sem("lru_conv_v"), ["tap1", "tap2", "tap3", "xc_lo"])
        lru_ca = Steps(sem("lru_conv_a"), ["tap0", "xc_hi"])
        lru_ya = Steps(sem("lru_y_a"), ["gelu"])
        lru_vn = ["ix0", "ix1", "q0", "q1", "b0", "scan0", "b1", "scan1", "rec", "z"]
        lru_v = Steps(sem("lru_v"), lru_vn, base=len(lru_vn))
        lru_a = Steps(sem("lru_a"), ["a0", "a1", "t0", "t1", "sq0", "sq1", "root0", "root1"])

        z_hi, z_lo = sem("z_hi"), sem("z_lo")
        src_hi, src_lo = sem("src_hi"), sem("src_lo")

        B_STEPS = ["u_b0", "p_b0", "u_b1", "p_b1", "lo_b0", "p_b2", "lo_b1", "lo_b2"]
        ffn_st = [(Steps(sem(f"f{n}_v"), ["p_a", "lo_a"] + B_STEPS),
                   Steps(sem(f"f{n}_a"), ["silu_a", "hi_a", "silu_b", "hi_b0", "hi_b1", "hi_b2"])) for n in range(2)]

        qkv_an, qkv_vn = [], []
        for j in range(HN):
            qkv_an += [f"g{j}"] + [f"swap{j}_{q}" for q in range(4)] + [f"sq{j}"]
        for j in range(HN + 2):
            if j - 2 >= HEADS:
                qkv_vn += [f"dup{j - 2}", f"klo{j - 2}"]
            if 1 <= j <= HN:
                qkv_vn += [f"rec{j - 1}"]
            if j < HN:
                qkv_vn += [f"cos{j}", f"sin{j}", f"rope{j}"]
        khi = Steps(sem("khi"), ["k"])
        qkv_a, qkv_v = Steps(sem("qkv_a"), qkv_an), Steps(sem("qkv_v"), qkv_vn)
        v_hi = Steps(sem("v_hi"), ["v"])

        def att_steps(tag, names, last):
            got = []
            for u in range(HEADS):
                for n in names:
                    ahead = {"mx": 2, "e": 1, "sum": 1, "rcp": 1}.get(n.rstrip("_").rstrip("012") if n[0] == "e" else n, 0)
                    if last and (n in ("qh", "ql") or u + ahead >= HEADS):
                        continue
                    got.append(f"{n}{u}")
            return Steps(sem(tag), got)

        A_NAMES = ("qh", "e0_", "e1_")
        V_NAMES = ("hi0_", "hi1_", "ql", "mx", "hi2_", "sum", "rcp")
        G_NAMES = ("lo0_", "lo1_", "lo2_")
        att_a, end_a = att_steps("att_a", A_NAMES, False), att_steps("att_end_a", A_NAMES, True)
        att_v, end_v = att_steps("att_v", V_NAMES, False), att_steps("att_end_v", V_NAMES, True)
        att_g = att_steps("att_g", G_NAMES, False)
        first_a = Steps(sem("att_first_a"), ["qh", "e0", "e1"])
        first_v = Steps(sem("att_first_v"), ["ql", "pad", "mx0", "sum0", "rcp0", "mx1"])

        def is_last(i):
            return isinstance(i, int) and i == QT - 1

        def max_done(k, i):
            if isinstance(i, int) and i == 0 and k < 2:
                return first_v.sem, first_v.after(f"mx{k}")
            if k < 2:
                return att_v.sem, att_v.after(f"mx{k + 6}", i - 1)
            st = end_v if is_last(i) else att_v
            return st.sem, st.after(f"mx{k - 2}", 0 if is_last(i) else i)

        def recip_done(k, i):
            if isinstance(i, int) and i == 0 and k < 1:
                return first_v.sem, first_v.after("rcp0")
            if k < 1:
                return att_v.sem, att_v.after("rcp7", i - 1)
            st = end_v if is_last(i) else att_v
            return st.sem, st.after(f"rcp{k - 1}", 0 if is_last(i) else i)

        def slice_done(k, i):
            if k >= HEADS:
                return att_v.sem, att_v.after(f"ql{k - HEADS}", i)
            if isinstance(i, int) and i == 0:
                return first_v.sem, first_v.after("ql")
            return att_v.sem, att_v.after(f"ql{k}", i - 1)

        rows = [slice(c * CW, (c + 1) * CW) for c in range(CHUNKS)]

        def chunked(tile):
            return tile.rearrange("p (c w) -> p c w", c=CHUNKS)

        def over_rows(tile, n):
            return tile.unsqueeze(1).broadcast_to([P, n, CW])

        def gain(layer, which, f):
            n = GAIN + (layer * 4 + which) * F + f
            return prm[:, n:n + 1]

        norms = [
            (0, None, 1, 2, None, (0, 0)),
            (3, 0, 1, 2, (0, 1), (0, 2)),
            (1, 0, 2, 3, (0, 3), (1, 0)),
            (0, 1, 2, 3, (1, 1), (1, 2)),
            (2, 1, None, None, (1, 3), None),
        ]

        def h_squares(t, c):
            return fr[3 if t == 0 else norms[t][1]][:, :, rows[c]]

        M_SPLIT = 4
        ffns = [(U_FFN0, J_FFN0, 1, 2, 3, 0, 1), (U_FFN1, J_FFN1, 2, 3, 0, 1, 2)]
        outs = [(U_LRU_OUT, J_LRU_OUT, 3, 1, 2, 0, 3), (U_ATT_OUT, J_ATT_OUT, 0, 2, 3, 1, 0)]

        def flat(region):
            return region[:, :, :].rearrange("p f t -> p (f t)")

        vhi = flat(rr[1])[:, 4 * TOKENS:4 * TOKENS + QT * 256].rearrange("p (k d) -> p k d", k=QT)
        PT = [[flat(rr[r])[:, kv * QT * GROUP * QW:(kv + 1) * QT * GROUP * QW]
               .rearrange("p (k h q) -> p k h q", k=QT, h=GROUP) for r in (2, 3)] for kv in range(KV_HEADS)]

        block = ctx.enter_context(nc.Block())

        @block.sync
        def _(eng):
            eng.dma_start(prm[:, :], params).then_inc(params_in, 16)

            def load(n, i=None):
                slot, turn = ring(n, WRING, i, WRING)
                wait(eng, w_ready[slot], turn)
                which = n if i is None else n + i * WRING
                eng.dma_start(raw[:, slot, :], weights[which, :, :]).then_inc(raw_full[slot], 16)

            for n in range(WRING):
                load(n)
            with eng.Fori(0, UNITS // WRING - 1) as i:
                for n in range(WRING):
                    load(n + WRING, i)
            for n in range(UNITS // WRING * WRING, UNITS):
                load(n)
            for c in range(CHUNKS):
                for f in range(0, F, 4):
                    eng.wait_ge(h_new, by_row(3, c, f + 3))
                    eng.dma_start(out[:, f:f + 4, rows[c]], fr[norms[4][0]][:, f:f + 4, rows[c]]).then_inc(out_done, 16)
            eng.wait_ge(out_done, 16 * CHUNKS * F // 4)

        @block.gpsimd
        def _(eng):
            nc.gpsimd.memset(ones[:, :], 1.0).then_inc(const_ready, 1)
            nc.gpsimd.memset(eps[:, :], EPS).then_inc(const_ready, 1)
            nc.gpsimd.memset(ident[:, :], 0.0).then_inc(const_ready, 1)
            eng.wait_ge(const_ready, 3)
            nc.gpsimd.affine_select(out=ident[:, :], in_=ident[:, :], compare_op=ALU.not_equal, fill=1.0, base=0,
                                    pattern=[[-1, P]], channel_multiplier=1).then_inc(const_ready, 1)

            def split(n, i=None):
                slot, turn = ring(n, WRING, i, WRING)
                first = isinstance(turn, int) and turn == 0
                wait(eng, raw_full[slot], 16 * (turn + 1))
                if not first:
                    wait(eng, w_free[slot], turn)
                eng.sem_inc(split_begun, 1)
                nc.gpsimd.tensor_scalar(whi[:, slot, :], raw[:, slot, :], 1.0, None, ALU.mult).then_inc(hi_done, 1)
                wait(eng, hi_done, n + 1 if i is None else n + i * WRING + 1)
                nc.gpsimd.tensor_tensor(wlo[:, slot, :], raw[:, slot, :], whi[:, slot, :].bitcast(F32),
                                        ALU.subtract).then_inc(w_ready[slot], 1)

            def units(a, b):
                turns = (b - a) // WRING
                if turns > 1:
                    with eng.Fori(0, turns) as i:
                        for n in range(WRING):
                            split(a + n, i)
                    a += turns * WRING
                for n in range(a, b):
                    split(n)

            def scale_m(t, c):
                m = norms[t][1]
                eng.wait_ge(aux_free[1], norm_turn(1, t, True, c) + 1)
                part = fr[m][:, M_SPLIT:F, rows[c]]
                nc.gpsimd.tensor_tensor(part, part, over_rows(rstd_m[:, c, :], F - M_SPLIT), ALU.mult).then_inc(scaled_g, 1)

            def z_low():
                src, hi, lo = outs[0][2:5]
                for f in range(F - 1):
                    eng.wait_ge(z_hi, f + 1)
                    nc.gpsimd.tensor_tensor(rr[lo][:, f, :], fr[src][:, f, :], rr[hi][:, f, :].bitcast(F32),
                                            ALU.subtract).then_inc(z_lo, 1)

            def fold(tile, n, by, done):
                nc.gpsimd.tensor_tensor(tile[:, 0:by, :], tile[:, 0:by, :], tile[:, n:n + by, :], ALU.add).then_inc(done, 1)

            def fold_m(t, c):
                layer = (t - 1) // 2
                eng.wait_ge(m_squared, len(LAST_ROWS) * by_chunk(layer, c) - 1)
                fold(squares, 3, 3, m_folded)
                eng.wait_ge(m_squared, len(LAST_ROWS) * by_chunk(layer, c))
                eng.wait_ge(m_folded, 2 * ((CHUNKS - 1) * layer + c) + 1)
                fold(squares, 6, 2, m_folded)

            def fold_h(t, c):
                eng.wait_ge(h_squared, by_chunk(t, c))
                fold(h_squares(t, c), 4, 4, h_folded)

            def attention_lo():
                def tile_steps(i):
                    for u in range(HEADS):
                        for t in range(CHUNKS):
                            st = end_v if is_last(i) else att_v
                            eng.wait_ge(st.sem, st.after(f"hi{t}_{u}", 0 if is_last(i) else i))
                            hi, lo = (PT[u // GROUP][x][0:QW, 3 * t:3 * t + 3, u % GROUP, :] for x in range(2))
                            att_g.did(f"lo{t}_{u}", nc.gpsimd.tensor_tensor(
                                lo, turn_f[0:QW, u % 2, t, :].rearrange("p (k q) -> p k q", k=3), hi.bitcast(F32), ALU.subtract))

                with eng.Fori(0, QT - 1) as i:
                    tile_steps(i)
                tile_steps(QT - 1)

            units(U_LRU, U_LRU + 2)
            fold_h(0, 0)
            split(U_LRU + 2)
            fold_h(0, 1)
            fold_h(0, 2)
            units(U_LRU + WRING, U_LRU_OUT + 2)
            z_low()
            units(U_LRU_OUT + 2, U_FFN0 + 1)

            def mixer_norm(t, u):
                scale_m(t, 0)
                split(u + 1)
                scale_m(t, 1)
                fold_h(t, 0)
                scale_m(t, 2)
                fold_h(t, 1)
                fold_h(t, 2)
                split(u + 2)

            mixer_norm(1, U_FFN0)
            units(U_FFN0 + 3, U_QKV + 1)
            fold_m(2, 0)
            fold_m(2, 1)
            scale_m(2, 0)
            scale_m(2, 1)
            split(U_QKV + 1)
            fold_h(2, 0)
            scale_m(2, 2)
            fold_h(2, 1)
            fold_h(2, 2)
            split(U_QKV + 2)
            units(U_QKV + 3, U_ATT_OUT + 1)
            attention_lo()
            units(U_ATT_OUT + 1, U_FFN1 + 1)
            mixer_norm(3, U_FFN1)
            units(U_FFN1 + 3, UNITS)
            fold_m(4, 0)
            fold_m(4, 1)
            scale_m(4, 0)
            scale_m(4, 1)
            scale_m(4, 2)

        @block.tensor
        def _(eng):
            held = []

            def mm(out_, lhs, rhs, start, stop):
                ins = nc.tensor.matmul(out_, lhs, rhs, start=start, stop=stop)
                return ins

            def free_held(ins):
                if held:
                    ins.then_inc(w_free[held.pop(0)], 1)

            def product(dst, todo, half_way=None):
                for k, (sh, sl, mh, ml) in enumerate(todo):
                    free_held(mm(dst, sh, mh, k == 0, False))
                    mm(dst, sh, ml, False, False)
                    last = mm(dst, sl, mh, False, k == len(todo) - 1)
                    if half_way is not None and k == len(todo) // 2 - 1:
                        half_way()
                return last

            def slot_free(n, i=None, per=0):
                slot, turn = main(n, i, per)
                wait(eng, main_free[slot], turn)
                return slot

            def unit_ready(u, i=None, per=0):
                s, t = ring(u, WRING, i, per)
                wait(eng, w_ready[s], t + 1)

            def job(n, i, per, parts, unit=(), unit_per=0, width=CW, behind=None):
                slot = slot_free(n, i, per)
                for u in unit:
                    unit_ready(u, i, unit_per)
                for c in range(CHUNKS):
                    todo = parts(c)
                    last = product(slots[slot][0:todo[0][0].shape[1], c, 0:width], todo)
                    if c == CHUNKS - 1:
                        last.then_inc(main_full[slot], 1)
                    if behind is not None:
                        behind(c)

            def from_u(u, hi, lo):
                s = u % WRING
                return lambda c: [(whi[:, s, k * P:(k + 1) * P], wlo[:, s, k * P:(k + 1) * P],
                                   rr[hi][:, k, rows[c]], rr[lo][:, k, rows[c]]) for k in range(F)]

            def release(*units):
                held.extend(u % WRING for u in units)

            def square_sum(turn, squared):
                wait(eng, aux_free[0], turn)
                for k in range(3):
                    for f, row in enumerate(squared):
                        ins = mm(banks[0][0:QW, k:k + 1], row[:, k * QW:(k + 1) * QW], ones[:, 0:1], f == 0,
                                 f == len(squared) - 1)
                ins.then_inc(aux_full[0], 1)

            def spread(turn, by_token, c):
                wait(eng, aux_free[1], turn)
                for k in range(3):
                    at = 3 * c + k
                    ins = nc.tensor.transpose(banks[1][:, k * QW:(k + 1) * QW],
                                              by_token[0:QW, at:at + 1].broadcast_to([QW, P]), ident[0:QW, 0:QW])
                ins.then_inc(aux_full[1], 1)

            def m_sum(t, c):
                layer = (t - 1) // 2
                if t in (1, 3):
                    s, turn = main(outs[layer][1] + OUT_ROWS + c)
                    eng.wait_ge(main_free[s], turn + 1)
                    eng.wait_ge(rows_summed, (OUT_ROWS - 1) * (layer + 1))
                    squared = [sumsq[:, rows[c]], squares[:, 0, :], squares[:, 1, :]]
                else:
                    eng.wait_ge(m_squared, len(LAST_ROWS) * by_chunk(layer, c))
                    if c < CHUNKS - 1:
                        eng.wait_ge(m_folded, 2 * ((CHUNKS - 1) * layer + c + 1))
                    else:
                        eng.wait_ge(m_folded_v, 2 * (layer + 1))
                    squared = [squares[:, f, :] for f in range(3)]
                square_sum(norm_turn(0, t, True, c), squared)

            def m_spread(t, c):
                eng.wait_ge(recip_m, by_chunk(t - 1, c))
                spread(norm_turn(1, t, True, c), rstd_t[:, 0, :], c)

            def h_sum(t, c):
                eng.wait_ge(h_folded, by_chunk(t, c))
                tile = h_squares(t, c)
                square_sum(norm_turn(0, t, False, c), [tile[:, f, :] for f in range(4)])

            def h_spread(t, c):
                eng.wait_ge(recip_h, by_chunk(t, c))
                spread(norm_turn(1, t, False, c), rstd_t[:, 1, :], c)

            def first_pair(t, n, u):
                parts = [from_u(u + k, norms[t][2], norms[t][3]) for k in range(2)]
                pair = [slot_free(n + k) for k in range(2)]

                def part(k, c, half_way=None):
                    eng.wait_ge(u_lo, by_row(t, c, F - 1))
                    if c == 0:
                        unit_ready(u + k)
                    last = product(slots[pair[k]][:, c, 0:CW], parts[k](c), half_way)
                    if c == CHUNKS - 1:
                        last.then_inc(main_full[pair[k]], 1)
                        release(u + k)

                if t == 0:
                    part(0, 0)
                    part(0, 1)
                    h_sum(t, 0)
                    part(0, 2)
                    h_sum(t, 1)
                    h_spread(t, 0)
                    h_sum(t, 2)
                    h_spread(t, 1)
                    part(1, 0)
                    h_spread(t, 2)
                    part(1, 1)
                    part(1, 2)
                    return
                part(0, 0)
                m_sum(t, CHUNKS - 1)
                part(1, 0)
                m_spread(t, CHUNKS - 1)
                part(0, 1)
                h_sum(t, 0)
                part(1, 1)
                part(0, 2)
                h_sum(t, 1)
                h_spread(t, 0)
                h_spread(t, 1)
                part(1, 2, lambda: h_sum(t, 2))
                h_spread(t, 2)

            eng.wait_ge(const_ready, 4)
            first_pair(0, J_LRU, U_LRU)

            def gates(i):
                s = (U_LRU + 2) % WRING
                eng.wait_ge(lru_cv.sem, lru_cv.after("xc_lo", i))
                for gate in range(4):
                    col = slice(gate * P, (gate + 1) * P)
                    job(J_LRU + 2 + gate, i, 6, lambda c: [(whi[:, s, col], wlo[:, s, col], xch[:, rows[c]], xcl[:, rows[c]])],
                        unit=[U_LRU + 2], unit_per=3)
                release(U_LRU + 2)

            with eng.Fori(0, F - 1) as i:
                gates(i)
                for k in range(2):
                    job(J_LRU + 6 + k, i, 6, from_u(U_LRU + 3 + k, 1, 2), unit=[U_LRU + 3 + k], unit_per=3)
                    release(U_LRU + 3 + k)
            gates(F - 1)

            def mixer_out(layer):
                u0, j0, src, hi, lo, m, back = outs[layer]
                t = 1 + 2 * layer
                parts = [from_u(u0 + n, hi, lo) for n in range(2)]
                pair = [slot_free(j0 + n) for n in range(2)]
                for k in range(F):
                    if layer == 0 and k < F - 1:
                        eng.wait_ge(z_lo, k + 1)
                    else:
                        eng.wait_ge(src_lo, 1 if layer == 0 else k + 2)
                    for n in range(2):
                        if k == 0:
                            unit_ready(u0 + n)
                        for c in range(CHUNKS):
                            sh, sl, mh, ml = parts[n](c)[k]
                            dst = slots[pair[n]][:, c, 0:CW]
                            free_held(mm(dst, sh, mh, k == 0, False))
                            mm(dst, sh, ml, False, False)
                            last = mm(dst, sl, mh, False, k == F - 1)
                        if k == F - 1:
                            last.then_inc(main_full[pair[n]], 1)
                release(u0, u0 + 1)
                for n in range(2, OUT_ROWS):
                    job(j0 + n, None, 0, from_u(u0 + n, hi, lo), unit=[u0 + n])
                    release(u0 + n)
                for c in range(CHUNKS):
                    slot = slot_free(j0 + OUT_ROWS + c)
                    for r in range(2):
                        u = u0 + OUT_ROWS + r
                        if c == 0:
                            unit_ready(u)
                        last = product(slots[slot][:, r, 0:CW], from_u(u, hi, lo)(c),
                                       (lambda: m_spread(t, c - 1)) if c and r else None)
                        if r == 1:
                            last.then_inc(main_full[slot], 1)
                        if c == CHUNKS - 1:
                            release(u)
                        if r == 0 and c:
                            m_sum(t, c - 1)

            def ffn(layer, t):
                u0, j0, hi, lo, mid, acc, back = ffns[layer]
                v = ffn_st[layer][0]

                def up(n, u, i=None):
                    job(j0 + n, i, 12, from_u(u0 + u, hi, lo), unit=[u0 + u], unit_per=6)
                    release(u0 + u)

                def hidden(u, f):
                    col = slice(f * P, (f + 1) * P)
                    return lambda c: [(whi[:, (u0 + u + k) % WRING, col], wlo[:, (u0 + u + k) % WRING, col],
                                       rr[mid][:, 2 * k, rows[c]], rr[mid][:, 2 * k + 1, rows[c]]) for k in range(2)]

                def down(n, u, i):
                    eng.wait_ge(v.sem, v.after("lo_b2", i))
                    for f in range(F):
                        job(j0 + n + f, i, 12, hidden(u, f), unit=[u0 + u, u0 + u + 1], unit_per=6)
                    release(u0 + u, u0 + u + 1)

                first_pair(t, j0, u0)
                up(2, 2)
                up(3, 3)
                with eng.Fori(0, FF // 2 - 1) as i:
                    up(4, 4, i)
                    up(5, 5, i)
                    down(6, 6, i)
                    up(14, 8, i)
                    up(15, 9, i)
                u = FFN_UNITS - 2
                unit_ready(u0 + u)
                unit_ready(u0 + u + 1)
                for c in range(CHUNKS):
                    eng.wait_ge(v.sem, v.after(f"lo_b{c}", FF // 2 - 1))
                    for g, (f0, f1) in enumerate(LAST_ROWS):
                        slot = slot_free(j0 + LAST_DOWN + c * len(LAST_ROWS) + g)
                        for f in range(f0, f1):
                            last = product(slots[slot][:, f - f0, 0:CW], hidden(u, f)(c))
                            if f == f1 - 1:
                                last.then_inc(main_full[slot], 1)
                            if c and g == 2 and f == f0:
                                m_spread(t + 1, c - 1)
                        if c and g == 1:
                            m_sum(t + 1, c - 1)
                release(u0 + u, u0 + u + 1)

            mixer_out(0)
            ffn(0, 1)

            chunks_done = [0]

            def head_norm_step(_):
                at = chunks_done[0]
                chunks_done[0] += 1
                j, c = at // CHUNKS, at % CHUNKS
                if c == 0 and 1 <= j <= HN:
                    head_spread(j - 1, CHUNKS - 1)
                if j < HN:
                    if c == 0:
                        eng.wait_ge(qkv_a.sem, qkv_a.after(f"sq{j}"))
                        turn = A_QKV[0] + j
                        wait(eng, aux_free[0], turn)
                        for k in range(QT):
                            ins = mm(banks[0][0:QW, k:k + 1], hsq[:, k * QW:(k + 1) * QW], ones[:, 0:1], True, True)
                        ins.then_inc(aux_full[0], 1)
                    else:
                        head_spread(j, c - 1)

            def head_spread(j, c):
                eng.wait_ge(qkv_v.sem, qkv_v.after(f"rec{j}"))
                spread(A_QKV[1] + j * CHUNKS + c, hrstd_t[:, :], c)

            first_pair(2, J_QKV, U_QKV)
            for j in range(2, HN):
                job(J_QKV + j, None, 0, from_u(U_QKV + j, 2, 3), unit=[U_QKV + j], behind=head_norm_step)
                release(U_QKV + j)
            uv = [U_QKV + HN, U_QKV + HN + 1]
            for t in range(VJOBS):
                def v_parts(c, t=t):
                    tok = slice((CHUNKS * t + c) * QW, (CHUNKS * t + c + 1) * QW)
                    parts = []
                    for k in range(F):
                        s = uv[k // 4] % WRING
                        col = slice((k % 4) * 256, (k % 4 + 1) * 256)
                        parts.append((rr[2][:, k, tok], rr[3][:, k, tok], whi[:, s, col], wlo[:, s, col]))
                    return parts

                job(J_QKV + HN + t, None, 0, v_parts, unit=uv, width=KV_HEADS * HEAD_DIM, behind=head_norm_step)
            release(*uv)

            def scores(k, c, i):
                slot, turn = main(J_ATT + k, i, HEADS) if not isinstance(i, int) else main(J_ATT + k + HEADS * i)
                if c == 0:
                    eng.wait_ge(*slice_done(k, i))
                    wait(eng, main_free[slot], turn)
                u = k % HEADS
                kv = u // GROUP
                dst = slots[slot][0:QW, c, 0:CW]
                kh, kl = rr[1][:, kv, rows[c]], rr[1][:, KV_HEADS + kv, rows[c]]
                free_held(mm(dst, qsh[:, u, :], kh, True, False))
                mm(dst, qsh[:, u, :], kl, False, False)
                ins = mm(dst, qsl[:, u, :], kh, False, True)
                if c == CHUNKS - 1:
                    ins.then_inc(main_full[slot], 1)

            def transposes(u, t, i):
                if t == 0:
                    slot, turn = main(J_ATT + u, i, HEADS) if not isinstance(i, int) else main(J_ATT + u + HEADS * i)
                    eng.wait_ge(main_free[slot], turn + 1)
                turn = turned(turned_unit(u, t), i)
                eng.wait_ge(aux_free[0], turn)
                for k in range(3):
                    kt = 3 * t + k
                    ins = nc.tensor.transpose(banks[0][0:QW, k * QW:(k + 1) * QW],
                                              prob[0:QW, u % 2, kt * QW:(kt + 1) * QW], ident[0:QW, 0:QW])
                ins.then_inc(aux_full[0], 1)

            def sums(kv, k, i, of):
                eng.wait_ge(aux_free[0], turned(k, i))
                for h in range(GROUP):
                    eng.wait_ge(*recip_done(kv * GROUP + h, of))
                    ins = nc.tensor.transpose(banks[0][:, h * QW:(h + 1) * QW],
                                              rsum[0:QW, kv * GROUP + h, :].broadcast_to([QW, P]), ident[0:QW, 0:QW])
                ins.then_inc(aux_full[0], 1)

            def values(kv, kts, i):
                for kt in kts:
                    if kt == 0:
                        eng.wait_ge(aux_free[1], summed(kv, i))
                    eng.wait_ge(att_g.sem, att_g.after(f"lo{kt // 3}_{(kv + 1) * GROUP - 1}", i))
                    dst = banks[1][:, 0:GROUP * QW]
                    cols = slice(kv * HEAD_DIM, (kv + 1) * HEAD_DIM)
                    mh, ml = (PT[kv][x][0:QW, kt, :, :].rearrange("p h q -> p (h q)") for x in range(2))
                    mm(dst, vhi[0:QW, kt, cols], mh, kt == 0, False)
                    mm(dst, vhi[0:QW, kt, cols], ml, False, False)
                    ins = mm(dst, vlo[0:QW, kt, cols], mh, False, kt == QT - 1)
                    if kt == QT - 1:
                        ins.then_inc(aux_full[1], 1)

            def tile_steps(i, first=False, last=False):
                for u in range(HEADS):
                    kv, of = (0, i) if u >= GROUP else (1, i - 1)
                    for t in range(CHUNKS):
                        if u + 2 < HEADS or not last:
                            scores(u + 2, t, i)
                        transposes(u, t, i)
                        if of is not i and first:
                            continue
                        values(kv, VALUES_AT[u % GROUP][t], of)
                    if u in SUMS_AFTER and not (first and u == 1):
                        sums(kv, SUMS_AFTER[u], i, of)

            eng.wait_ge(qkv_v.sem, qkv_v.after(f"klo{HN - 1}"))
            for u in range(2):
                for c in range(CHUNKS):
                    scores(u, c, 0)
            s, t = main(J_QKV + HN + VJOBS - 1)
            eng.wait_ge(main_free[s], t + 1)
            tile_steps(0, first=True)
            with eng.Fori(1, QT - 1) as i:
                tile_steps(i)
            tile_steps(QT - 1, last=True)
            values(1, range(QT), QT - 1)
            sums(1, TURNED, QT - 1, QT - 1)

            mixer_out(1)
            ffn(1, 3)
            m_sum(4, CHUNKS - 1)
            m_spread(4, CHUNKS - 1)

        @block.scalar
        def _(eng):
            act = nc.scalar.activation

            def full(n, i=None, per=0):
                s, t = main(n, i, per)
                eng.wait_ge(main_full[s], t + 1)
                return s

            def root(turn, dst, width, scale):
                eng.wait_ge(aux_full[0], turn + 1)
                act(dst, banks[0][0:QW, 0:width], ACT.Sqrt, bias=eps[0:QW, 0:1], scale=scale).then_inc(aux_free[0], 1)

            def m_root(t, c):
                root(norm_turn(0, t, True, c), root_t[0:QW, 0, 3 * c:3 * c + 3], 3, 1.0 / D_MODEL)

            def h_root(t, c):
                root(norm_turn(0, t, False, c), root_t[0:QW, 1, 3 * c:3 * c + 3], 3, 1.0 / D_MODEL)

            def m_out(t, c):
                turn = norm_turn(1, t, True, c)
                eng.wait_ge(aux_full[1], turn + 1)
                act(rstd_m[:, c, :], banks[1][:, 0:CW], ACT.Copy).then_inc(aux_free[1], 1)

            def h_out(t, c):
                turn = norm_turn(1, t, False, c)
                eng.wait_ge(aux_full[1], turn + 1)
                act(rstd[:, c, :], banks[1][:, 0:CW], ACT.Copy).then_inc(aux_free[1], 1)

            def high(t, c):
                h, m, hi, lo, g1, g0 = norms[t]
                for f in range(F):
                    if t > 0:
                        eng.wait_ge(h_new, by_row(t - 1, c, f))
                    elif f == 0:
                        eng.wait_ge(h_in[c], 16)
                    act(rr[hi][:, f, rows[c]], fr[h][:, f, rows[c]], ACT.Identity, scale=gain(*g0, f)).then_inc(u_hi, 1)
                if t > 0:
                    eng.dma_start(spill[:, :, rows[c]], fr[h][:, :, rows[c]]).then_inc(h_spilled, 16)

            def square_h(t, c):
                act(h_squares(t, c), fr[norms[t][0]][:, :, rows[c]], ACT.Square).then_inc(h_squared, 1)

            def norm(t):
                if t == 0:
                    high(t, 0)
                high(t, 1)
                if t > 0:
                    m_root(t, 2)
                square_h(t, 0)
                if t > 0:
                    m_out(t, 2)
                if t == 0:
                    high(t, 2)
                square_h(t, 1)
                if t > 0:
                    high(t, 2)
                square_h(t, 2)
                for c in range(CHUNKS):
                    h_root(t, c)
                    h_out(t, c)

            for c in range(CHUNKS):
                eng.dma_start(fr[0][:, :, rows[c]], h0[:, :, rows[c]]).then_inc(h_in[c], 16)
            eng.wait_ge(sp_v.sem, 1)
            sp_a.did("exp", act(sp[:, 1, :], sp[:, 0, :], ACT.Exp, scale=-1.0))
            eng.wait_ge(const_ready, 4)
            eng.wait_ge(params_in, 16)
            norm(0)
            rt = fr[0]

            def convolve(i, n):
                v, a = lru_cv, lru_ca
                s, t = main(J_LRU + 6 * n, i, 6)
                eng.wait_ge(main_free[s], t + 1)
                if n:
                    eng.wait_ge(v.sem, v.after("xc_lo", i))
                    eng.wait_ge(lru_v.sem, lru_v.after("ix1", i))
                a.did("tap0", act(xc[:, :], xpad[:, 0:TOKENS], ACT.Identity, bias=prm[:, bass.ds(i + (CONVB + n), 1)],
                                  scale=prm[:, bass.ds(i + (CONVW + n), 1)]))

            def x_high(i, n):
                v, a = lru_cv, lru_ca
                eng.wait_ge(v.sem, v.after("tap3", i) + n * len(v.names))
                a.did("xc_hi", act(xch[:, :], xc[:, :], ACT.Copy))

            def gates(i):
                v, a = lru_v, lru_a

                def before(name):
                    eng.wait_ge(v.sem, v.after(name, i) - len(lru_vn))

                for g, reader in enumerate(("q0", "b0", "q1", "b1")):
                    s = full(J_LRU + 2 + g, i, 6)
                    before(reader)
                    act(chunked(rt[:, g, :]), slots[s][:, :, 0:CW], ACT.Sigmoid,
                        bias=prm[:, bass.ds(i + (GATEB + g * F), 1)]).then_inc(main_free[s], 1)
                s, t = main(J_LRU + 1, i, 6)
                eng.wait_ge(main_free[s], t + 1)
                lru_ya.did("gelu", act(fr[3][:, i, :], fr[3][:, i, :], ACT.Gelu_apprx_tanh))
                for d in range(2):
                    s, t = main(J_LRU + 2 + 2 * d, i, 6)
                    eng.wait_ge(main_free[s], t + 1)
                    before(f"scan{d}")
                    a.did(f"a{d}", act(rt[:, 4 + d, :], rt[:, 2 * d, :], ACT.Exp, scale=sp[:, 4, bass.ds(i + d * F, 1)]))
                for d in range(2):
                    eng.wait_ge(a.sem, a.after(f"a{d}", i))
                    a.did(f"t{d}", act(rt[:, 2 * d, :], rt[:, 2 * d, :], ACT.Tanh, scale=sp[:, 5, bass.ds(i + d * F, 1)]))
                before("z")
                for d in range(2):
                    a.did(f"sq{d}", act(rt[:, 6 + d, :], rt[:, 4 + d, :], ACT.Square))

            def roots(i):
                v, a = lru_v, lru_a
                for d in range(2):
                    eng.wait_ge(v.sem, v.after(f"q{d}", i))
                    a.did(f"root{d}", act(rt[:, 6 + d, :], rt[:, 6 + d, :], ACT.Sqrt))

            eng.wait_ge(sp_v.sem, sp_v.after("s22"))
            eng.wait_ge(u_lo, by_row(0, CHUNKS - 1, F - 1))
            convolve(0, 0)
            x_high(0, 0)
            with eng.Fori(0, F - 1) as i:
                gates(i)
                convolve(i, 1)
                roots(i)
                x_high(i, 1)
            gates(F - 1)
            roots(F - 1)

            def mixer_out(layer):
                u0, j0, src, hi, lo, m, back = outs[layer]
                t = 1 + 2 * layer

                def source_high(f):
                    act(rr[hi][:, f, :], fr[src][:, f, :], ACT.Copy).then_inc(src_hi, 1)

                if layer == 0:
                    eng.wait_ge(lru_v.sem, lru_v.after("z", F - 1))
                    source_high(F - 1)
                    eng.wait_ge(z_lo, F - 1)
                    eng.wait_ge(src_lo, 1)
                    eng.dma_start(fr[back][:, :, :], h0).then_inc(h_back, 16)
                else:
                    eng.wait_ge(aux_free[1], summed(0, QT - 1) + 1)
                    for f in range(GROUP):
                        source_high(f)
                    sums(TURNED, QT - 1, False)
                    eng.wait_ge(aux_free[1], summed(1, QT - 1) + 1)
                    for f in range(GROUP, HEADS):
                        source_high(f)
                    eng.wait_ge(src_lo, 1 + F)
                    eng.wait_ge(h_spilled, 16 * CHUNKS * 2)
                    eng.dma_start(fr[back][:, :, :], spill).then_inc(h_back, 16)
                for n in range(OUT_ROWS):
                    s = full(j0 + n)
                    act(chunked(fr[m][:, n, :]), slots[s][:, :, 0:CW], ACT.Copy)
                    if n > 1:
                        eng.wait_ge(rows_summed, (OUT_ROWS - 1) * layer + n - 1)
                    act(chunked(sqtile[:, :] if n else sumsq[:, :]), slots[s][:, :, 0:CW], ACT.Square).then_inc(main_free[s], 1)

                def last_rows(c):
                    s = full(j0 + OUT_ROWS + c)
                    act(fr[m][:, OUT_ROWS:F, rows[c]], slots[s][:, 0:2, 0:CW], ACT.Copy)
                    act(squares[:, 0:2, :], slots[s][:, 0:2, 0:CW], ACT.Square).then_inc(main_free[s], 1)

                last_rows(0)
                m_root(t, 0)
                m_out(t, 0)
                last_rows(1)
                m_root(t, 1)
                high(t, 0)
                m_out(t, 1)
                last_rows(2)

            def ffn(layer):
                u0, j0, hi, lo, mid, acc, back = ffns[layer]
                v, a = ffn_st[layer]
                t = 2 + 2 * layer

                def hidden(x, n, i, turn):
                    s, tt = main(j0 + n, i, 12)
                    eng.wait_ge(main_free[s], tt + 1)
                    if turn is not None:
                        eng.wait_ge(v.sem, v.after("p_b2", turn - 1) if x == "a" else v.after("p_a", turn))
                    turn = 0 if turn is None else turn
                    a.did(f"silu_{x}", act(fr[mid][:, 4, :], fr[mid][:, 6, :], ACT.Silu))
                    if x == "a" and i is not None:
                        full(j0 + 13, i, 12)
                    if x == "a":
                        eng.wait_ge(v.sem, v.after("p_a", turn))
                        a.did("hi_a", act(rr[mid][:, 0, :], fr[mid][:, 5, :], ACT.Copy))
                    else:
                        for c in range(CHUNKS):
                            eng.wait_ge(v.sem, v.after(f"p_b{c}", turn))
                            a.did(f"hi_b{c}", act(rr[mid][:, 2, rows[c]], fr[mid][:, 5, rows[c]], ACT.Copy))

                hidden("a", 0, None, None)
                hidden("b", 2, None, 0)
                with eng.Fori(0, FF // 2 - 1) as i:
                    hidden("a", 4, i, i + 1)
                    hidden("b", 14, i, i + 1)
                eng.wait_ge(h_spilled, 16 * CHUNKS * (1 + 2 * layer))
                eng.dma_start(fr[back][:, :, :], spill).then_inc(h_back, 16)

                def square_m(c, g):
                    f0, f1 = LAST_ROWS[g]
                    s, turn = main(j0 + LAST_DOWN + c * len(LAST_ROWS) + g)
                    eng.wait_ge(main_free[s], turn + 1)
                    act(squares[:, f0:f1, :], fr[acc][:, f0:f1, rows[c]], ACT.Square).then_inc(m_squared, 1)

                for g in range(3):
                    square_m(0, g)
                m_root(t, 0)
                square_m(1, 0)
                square_m(1, 1)
                m_out(t, 0)
                square_m(1, 2)
                m_root(t, 1)
                if norms[t][2] is not None:
                    high(t, 0)
                    m_out(t, 1)
                square_m(2, 0)
                square_m(2, 1)
                if norms[t][2] is None:
                    m_out(t, 1)
                square_m(2, 2)

            mixer_out(0)
            norm(1)
            ffn(0)
            norm(2)

            eng.dma_start(cossin[:, :, :], rope).then_inc(tables_in, 16)
            eng.wait_ge(h_spilled, 16 * CHUNKS * 2)
            a, v = qkv_a, qkv_v

            def head_root(j):
                if j:
                    eng.wait_ge(v.sem, v.after(f"rec{j - 1}"))
                root(A_QKV[0] + j, hroot_t[0:QW, :], QT, 1.0 / HEAD_DIM)

            def k_high(j):
                eng.wait_ge(v.sem, v.after(f"dup{j}"))
                khi.did("k", act(rr[1][:, j - HEADS, :], fr[1][:, 2 + j - HEADS, :], ACT.Copy))

            def v_high(t):
                s = full(J_QKV + HN + t)
                for k in range(3):
                    tile = 3 * t + k
                    v_hi.did("v", act(vhi[0:QW, tile, :], slots[s][0:QW, k, 0:256], ACT.Identity,
                                      scale=rstd_t[0:QW, 1, tile:tile + 1]))

            for j in range(HN):
                s, t = main(J_QKV + j)
                g = QGAIN if j < HEADS else KGAIN
                eng.wait_ge(main_free[s], t + 1)
                if j:
                    eng.wait_ge(v.sem, v.after(f"rope{j - 1}"))
                a.did(f"g{j}", act(hg[:, :], hraw[:, :], ACT.Identity, scale=prm[:, g:g + 1]))
                eng.wait_ge(a.sem, a.after(f"g{j}"))
                for q in range(4):
                    if j and q == 3:
                        head_root(j - 1)
                    a.did(f"swap{j}_{q}", act(hs[32 * q:32 * q + 32, :], hg[32 * (q ^ 1):32 * (q ^ 1) + 32, :], ACT.Copy))
                a.did(f"sq{j}", act(hsq[:, :], hraw[:, :], ACT.Square))
            v_high(0)
            head_root(HN - 1)
            k_high(HN - 2)
            v_high(1)
            k_high(HN - 1)
            v_high(2)

            eng.wait_ge(qkv_v.sem, qkv_v.after(f"klo{HN - 1}"))
            first_a.did("qh", act(qsh[:, :, :], fr[0][:, :, 0:QW], ACT.Copy))

            def exp(k, c, i, did):
                slot, _ = main(J_ATT + k, i, HEADS) if not isinstance(i, int) else main(J_ATT + k + HEADS * i)
                b = k % 2
                w = CW if c < CHUNKS - 1 else CW - PAD
                if c == 0:
                    eng.wait_ge(*max_done(k, i))
                ins = act(prob[0:QW, b, c * CW:c * CW + w], slots[slot][0:QW, c, 0:w], ACT.Exp, bias=stat[0:QW, b, 0:1],
                          scale=-1.0, accum_out=stat[0:QW, b, 1 + c:2 + c])
                if c == CHUNKS - 1:
                    ins.then_inc(main_free[slot], 1)
                else:
                    did(ins)

            def tile_steps(i, first=False, last=False):
                a = end_a if last else att_a
                for u in range(HEADS):
                    if not last:
                        a.did(f"qh{u}", act(qsh[:, u, :], fr[0][:, u, bass.ds(i * QW + QW, QW)], ACT.Copy))
                    def out_of_bank(t):
                        turn = turned(turned_unit(u, t), i)
                        eng.wait_ge(aux_full[0], turn + 1)
                        if t == 0 and not (first and u < 2):
                            eng.wait_ge(att_g.sem, att_g.after(f"lo2_{(u - 2) % HEADS}", i if u >= 2 else i - 1))
                        act(turn_f[0:QW, u % 2, t, :], banks[0][0:QW, 0:CW], ACT.Copy).then_inc(aux_free[0], 1)

                    for what, t in (("T", 0), ("E", 0), ("T", 1), ("E", 1), ("E", 2), ("T", 2)):
                        if what == "T":
                            out_of_bank(t)
                        elif u + 1 < HEADS or not last:
                            exp(u + 1, t, i, lambda ins: a.did(f"e{t}_{u}", ins))
                    if u in SUMS_AFTER and not (first and u == 1):
                        sums(SUMS_AFTER[u], i, u == 5 and first)

            def sums(k, i, none_before):
                eng.wait_ge(aux_full[0], turned(k, i) + 1)
                if not none_before:
                    kv, of = (1, i - 1) if k == SUMS_AFTER[5] else (0, i - 1)
                    if k == TURNED:
                        kv, of = 0, i
                    eng.wait_ge(aux_free[1], summed(kv, of) + 1)
                act(recips[:, :], banks[0][:, 0:GROUP * QW], ACT.Copy).then_inc(aux_free[0], 1)

            for c in range(CHUNKS):
                exp(0, c, 0, lambda ins: first_a.did(f"e{c}", ins))
            tile_steps(0, first=True)
            with eng.Fori(1, QT - 1) as i:
                tile_steps(i)
            tile_steps(QT - 1, last=True)

            mixer_out(1)
            norm(3)
            ffn(1)
            m_root(4, CHUNKS - 1)
            m_out(4, CHUNKS - 1)

        @block.vector
        def _(eng):
            vec = nc.vector

            def full(n, i=None, per=0):
                s, t = main(n, i, per)
                eng.wait_ge(main_full[s], t + 1)
                return s

            count = [0]

            def link(ins):
                sp_v.did(f"s{count[0]}", ins)
                count[0] += 1
                eng.wait_ge(sp_v.sem, count[0])

            eng.wait_ge(params_in, 16)
            lam = prm[:, LAM:LAM + 2 * F]
            link(vec.scalar_tensor_tensor(out=sp[:, 0, :], in0=lam, scalar=-1.0, in1=lam, op0=ALU.mult, op1=ALU.max))
            eng.wait_ge(sp_a.sem, 1)
            link(vec.tensor_scalar(sp[:, 2, :], sp[:, 1, :], 2.0, None, ALU.add))
            link(vec.reciprocal(sp[:, 3, :], sp[:, 2, :]))
            link(vec.tensor_tensor(sp[:, 0, :], sp[:, 1, :], sp[:, 3, :], ALU.mult))
            link(vec.tensor_tensor(sp[:, 1, :], sp[:, 0, :], sp[:, 0, :], ALU.mult))
            link(vec.tensor_scalar(sp[:, 2, :], sp[:, 1, :], 1.0 / 15, 1.0 / 13, ALU.mult, ALU.add))
            for d in (11, 9, 7, 5, 3, 1):
                link(vec.tensor_tensor(sp[:, 3, :], sp[:, 2, :], sp[:, 1, :], ALU.mult))
                link(vec.tensor_scalar(sp[:, 2, :], sp[:, 3, :], 1.0 / d, None, ALU.add))
            link(vec.tensor_tensor(sp[:, 3, :], sp[:, 2, :], sp[:, 0, :], ALU.mult))
            link(vec.tensor_scalar(sp[:, 0, :], lam, -1.0, 0.0, ALU.mult, ALU.max))
            link(vec.scalar_tensor_tensor(out=sp[:, 2, :], in0=sp[:, 3, :], scalar=2.0, in1=sp[:, 0, :],
                                          op0=ALU.mult, op1=ALU.add))
            link(vec.tensor_scalar(sp[:, 4, :], sp[:, 2, :], -LRU_C, None, ALU.mult))
            link(vec.tensor_scalar(sp[:, 5, :], sp[:, 2, :], LRU_C, None, ALU.mult))

            def recip(t, of_m, c):
                x = 0 if of_m else 1
                at = slice(3 * c, 3 * c + 3)
                eng.wait_ge(aux_free[0], norm_turn(0, t, of_m, c) + 1)
                vec.reciprocal(rstd_t[0:QW, x, at], root_t[0:QW, x, at]).then_inc(recip_m if of_m else recip_h, 1)

            def scale_m(t, c):
                m = norms[t][1]
                eng.wait_ge(aux_free[1], norm_turn(1, t, True, c) + 1)
                part = fr[m][:, 0:M_SPLIT, rows[c]]
                vec.tensor_tensor(part, part, over_rows(rstd_m[:, c, :], M_SPLIT), ALU.mult).then_inc(scaled_v, 1)

            def update(t, c, f0=0, f1=F):
                h, m, hi, lo, g1, g0 = norms[t]
                for f in range(f0, f1):
                    if f == 0:
                        eng.wait_ge(scaled_v, by_chunk(t - 1, c))
                        if c == 0:
                            eng.wait_ge(h_back, 16 * t)
                    if f == M_SPLIT:
                        eng.wait_ge(scaled_g, by_chunk(t - 1, c))
                    vec.scalar_tensor_tensor(out=fr[h][:, f, rows[c]], in0=fr[m][:, f, rows[c]], scalar=gain(*g1, f),
                                             in1=fr[h][:, f, rows[c]], op0=ALU.mult, op1=ALU.add).then_inc(h_new, 1)

            def low(t, c):
                h, m, hi, lo, g1, g0 = norms[t]
                for f in range(F):
                    eng.wait_ge(u_hi, by_row(t, c, f))
                    vec.scalar_tensor_tensor(out=rr[lo][:, f, rows[c]], in0=fr[h][:, f, rows[c]], scalar=gain(*g0, f),
                                             in1=rr[hi][:, f, rows[c]].bitcast(F32), op0=ALU.mult,
                                             op1=ALU.subtract).then_inc(u_lo, 1)

            def norm(t):
                if t == 0:
                    low(t, 0)
                else:
                    scale_m(t, 1)
                    update(t, 1)
                low(t, 1)
                if t > 0:
                    recip(t, True, 2)
                    scale_m(t, 2)
                    update(t, 2)
                low(t, 2)
                for c in range(CHUNKS):
                    recip(t, False, c)

            norm(0)

            rt = fr[0]
            vec.memset(xpad[:, 0:CONV_LEFT], 0.0)
            vec.memset(xpad[:, CONV_LEFT + TOKENS:], 0.0).then_inc(lru_v.sem, len(lru_vn))

            def x_in(i, n):
                if n:
                    eng.wait_ge(lru_cv.sem, lru_cv.after("tap3", i))
                else:
                    eng.wait_ge(aux_free[1], norm_turn(1, 0, False, CHUNKS - 1) + 1)
                s = full(J_LRU + 6 * n, i, 6)
                vec.tensor_tensor(chunked(xpad[:, CONV_LEFT:CONV_LEFT + TOKENS]), slots[s][:, :, 0:CW], rstd[:, :, :],
                                  ALU.mult).then_inc(main_free[s], 1)

            def taps(i, n):
                v, a = lru_cv, lru_ca
                eng.wait_ge(a.sem, a.after("tap0", i) + n * len(a.names))
                for k in range(1, CONV_W):
                    if k > 1:
                        eng.wait_ge(v.sem, v.after(f"tap{k - 1}", i) + n * len(v.names))
                    v.did(f"tap{k}", vec.scalar_tensor_tensor(
                        out=xc[:, :], in0=xpad[:, k:k + TOKENS], scalar=prm[:, bass.ds(i + (CONVW + k * F + n), 1)],
                        in1=xc[:, :], op0=ALU.mult, op1=ALU.add))

            def x_low(i, n):
                v, a = lru_cv, lru_ca
                eng.wait_ge(a.sem, a.after("xc_hi", i) + n * len(a.names))
                v.did("xc_lo", vec.tensor_tensor(xcl[:, :], xc[:, :], xch[:, :].bitcast(F32), ALU.subtract))

            def y_in(i, n):
                s = full(J_LRU + 1 + 6 * n, i, 6)
                row = fr[3][:, bass.ds(i + n, 1), :] if not isinstance(i, int) else fr[3][:, i + n:i + n + 1, :]
                vec.tensor_tensor(row.rearrange("p o (c w) -> p (o c) w", c=CHUNKS), slots[s][:, :, 0:CW], rstd[:, :, :],
                                  ALU.mult).then_inc(main_free[s], 1)

            def inputs(i):
                v = lru_v
                for d in range(2):
                    s, t = main(J_LRU + 3 + 2 * d, i, 6)
                    eng.wait_ge(main_free[s], t + 1)
                    v.did(f"ix{d}", vec.tensor_tensor(rt[:, 1 + 2 * d, :], rt[:, 1 + 2 * d, :], xc[:, :], ALU.mult))

            def complements(i):
                v, a = lru_v, lru_a
                for d in range(2):
                    eng.wait_ge(a.sem, a.after(f"sq{d}", i))
                    v.did(f"q{d}", vec.scalar_tensor_tensor(out=rt[:, 6 + d, :], in0=rt[:, 6 + d, :], scalar=1.0,
                                                            in1=rt[:, 2 * d, :], op0=ALU.add, op1=ALU.mult))

            def drive(d, i):
                v, a = lru_v, lru_a
                eng.wait_ge(a.sem, a.after(f"root{d}", i))
                v.did(f"b{d}", vec.tensor_tensor(rt[:, 6 + d, :], rt[:, 6 + d, :], rt[:, 1 + 2 * d, :], ALU.mult))

            def scan(d, i):
                v = lru_v
                eng.wait_ge(v.sem, v.after(f"b{d}", i))
                way = (lambda x: x[:, 0:REAL]) if d == 0 else (lambda x: x[:, REAL - 1::-1])
                v.did(f"scan{d}", vec.tensor_tensor_scan(way(rt[:, 6 + d, :]), way(rt[:, 4 + d, :]), way(rt[:, 6 + d, :]),
                                                         0.0, ALU.mult, ALU.add))

            def combine(i):
                v = lru_v
                eng.wait_ge(v.sem, v.after("scan1", i))
                v.did("rec", vec.tensor_tensor(rt[:, 6, :], rt[:, 6, :], rt[:, 7, :], ALU.add))
                eng.wait_ge(v.sem, v.after("rec", i))
                eng.wait_ge(lru_ya.sem, lru_ya.after("gelu", i))
                v.did("z", vec.tensor_tensor(fr[3][:, i, :], fr[3][:, i, :], rt[:, 6, :], ALU.mult))

            def z_high():
                s, t = main(J_LRU + 1 + 6 * (F - 1))
                eng.wait_ge(main_full[s], t + 1)
                eng.wait_ge(lru_v.sem, lru_v.after("z", F - 2))
                hi = rr[outs[0][3]]
                for f in range(F - 1):
                    vec.tensor_copy(hi[:, f, :], fr[3][:, f, :]).then_inc(z_hi, 1)

            x_in(0, 0)
            taps(0, 0)
            x_low(0, 0)
            y_in(0, 0)
            with eng.Fori(0, F - 1) as i:
                inputs(i)
                x_in(i, 1)
                complements(i)
                taps(i, 1)
                drive(0, i)
                x_low(i, 1)
                scan(0, i)
                y_in(i, 1)
                drive(1, i)
                scan(1, i)
                combine(i)
            z_high()
            inputs(F - 1)
            complements(F - 1)
            for d in range(2):
                drive(d, F - 1)
                scan(d, F - 1)
            combine(F - 1)

            def source_low(layer, f):
                src, hi, lo = outs[layer][2:5]
                eng.wait_ge(src_hi, 1 if layer == 0 else f + 2)
                vec.tensor_tensor(rr[lo][:, f, :], fr[src][:, f, :], rr[hi][:, f, :].bitcast(F32), ALU.subtract).then_inc(src_lo, 1)

            def mixer_out(layer):
                u0, j0, src, hi, lo, m, back = outs[layer]
                t = 1 + 2 * layer
                for n in range(1, OUT_ROWS):
                    s, turn = main(j0 + n)
                    eng.wait_ge(main_free[s], turn + 1)
                    if n > 1:
                        eng.wait_ge(rows_summed, (OUT_ROWS - 1) * layer + n - 1)
                    vec.tensor_tensor(sumsq[:, :], sumsq[:, :], sqtile[:, :], ALU.add).then_inc(rows_summed, 1)
                recip(t, True, 0)
                scale_m(t, 0)
                update(t, 0, 0, 6)
                recip(t, True, 1)
                update(t, 0, 6, F)
                low(t, 0)

            def ffn(layer):
                u0, j0, hi, lo, mid, acc, back = ffns[layer]
                v, a = ffn_st[layer]
                t = 2 + 2 * layer

                def gate_in(x, n, i, turn):
                    s = full(j0 + n, i, 12)
                    if turn is not None:
                        eng.wait_ge(a.sem, a.after("silu_b", turn - 1) if x == "a" else a.after("silu_a", turn))
                    vec.tensor_tensor(chunked(fr[mid][:, 6, :]), slots[s][:, :, 0:CW], rstd[:, :, :], ALU.mult).then_inc(main_free[s], 1)

                def hidden_a(n, i, turn):
                    gate_in("a", n, i, turn)
                    s, tt = main(j0 + n + 1, i, 12)
                    full(j0 + n + 1, i, 12)
                    if turn is not None:
                        eng.wait_ge(v.sem, v.after("lo_b2", turn - 1))
                    turn = 0 if turn is None else turn
                    vec.tensor_tensor(chunked(fr[mid][:, 7, :]), slots[s][:, :, 0:CW], rstd[:, :, :], ALU.mult).then_inc(main_free[s], 1)
                    eng.wait_ge(main_free[s], tt + 1)
                    eng.wait_ge(a.sem, a.after("silu_a", turn))
                    v.did("p_a", vec.tensor_tensor(fr[mid][:, 5, :], fr[mid][:, 7, :], fr[mid][:, 4, :], ALU.mult))

                def low_a(turn):
                    eng.wait_ge(a.sem, a.after("hi_a", turn))
                    v.did("lo_a", vec.tensor_tensor(rr[mid][:, 1, :], fr[mid][:, 5, :], rr[mid][:, 0, :].bitcast(F32), ALU.subtract))

                def hidden_b(n, i, turn):
                    gate_in("b", n, i, turn)
                    s, tt = main(j0 + n + 1, i, 12)
                    full(j0 + n + 1, i, 12)
                    eng.wait_ge(v.sem, v.after("lo_a", turn))

                    def up_in(c):
                        return vec.tensor_tensor(fr[mid][:, 7, rows[c]], slots[s][:, c, 0:CW], rstd[:, c, :], ALU.mult)

                    def multiply(c):
                        if c < CHUNKS - 1:
                            eng.wait_ge(v.sem, v.after(f"u_b{c}", turn))
                        else:
                            eng.wait_ge(main_free[s], tt + 1)
                        if c == 0:
                            eng.wait_ge(a.sem, a.after("silu_b", turn))
                        v.did(f"p_b{c}", vec.tensor_tensor(fr[mid][:, 5, rows[c]], fr[mid][:, 7, rows[c]],
                                                           fr[mid][:, 4, rows[c]], ALU.mult))

                    def low(c):
                        eng.wait_ge(a.sem, a.after(f"hi_b{c}", turn))
                        v.did(f"lo_b{c}", vec.tensor_tensor(rr[mid][:, 3, rows[c]], fr[mid][:, 5, rows[c]],
                                                            rr[mid][:, 2, rows[c]].bitcast(F32), ALU.subtract))

                    v.did("u_b0", up_in(0))
                    multiply(0)
                    v.did("u_b1", up_in(1))
                    multiply(1)
                    low(0)
                    up_in(2).then_inc(main_free[s], 1)
                    multiply(2)
                    low(1)
                    low(2)

                def add(n, f, i):
                    s = full(j0 + n, i, 12)
                    vec.tensor_tensor(chunked(fr[acc][:, f, :]), slots[s][:, :, 0:CW], chunked(fr[acc][:, f, :]),
                                      ALU.add).then_inc(main_free[s], 1)

                eng.wait_ge(h_spilled, 16 * CHUNKS * (1 + 2 * layer))
                eng.wait_ge(u_lo, by_row(t - 1, CHUNKS - 1, F - 1))
                eng.wait_ge(aux_free[1], norm_turn(1, t - 1, False, CHUNKS - 1) + 1)
                hidden_a(0, None, None)
                low_a(0)
                vec.memset(fr[acc][:, :, :], 0.0).then_inc(zero, 1)
                hidden_b(2, None, 0)
                eng.wait_ge(zero, 1 + layer)
                with eng.Fori(0, FF // 2 - 1) as i:
                    hidden_a(4, i, i + 1)
                    for f in range(F):
                        add(6 + f, f, i)
                    low_a(i + 1)
                    hidden_b(14, i, i + 1)

                def add_rows(c, g):
                    f0, f1 = LAST_ROWS[g]
                    s = full(j0 + LAST_DOWN + c * len(LAST_ROWS) + g)
                    part = fr[acc][:, f0:f1, rows[c]]
                    vec.tensor_tensor(part, slots[s][:, 0:f1 - f0, 0:CW], part, ALU.add).then_inc(main_free[s], 1)

                for g in range(3):
                    add_rows(0, g)
                add_rows(1, 0)
                add_rows(1, 1)
                recip(t, True, 0)
                add_rows(1, 2)
                scale_m(t, 0)
                add_rows(2, 0)
                update(t, 0, 0, 4)
                add_rows(2, 1)
                update(t, 0, 4, 6)
                recip(t, True, 1)
                update(t, 0, 6, F)
                add_rows(2, 2)
                if norms[t][2] is not None:
                    low(t, 0)
                eng.wait_ge(m_squared, len(LAST_ROWS) * by_chunk(layer, CHUNKS - 1) - 1)
                vec.tensor_tensor(squares[:, 0:3, :], squares[:, 0:3, :], squares[:, 3:6, :], ALU.add).then_inc(m_folded_v, 1)
                eng.wait_ge(m_squared, len(LAST_ROWS) * by_chunk(layer, CHUNKS - 1))
                eng.wait_ge(m_folded_v, 2 * layer + 1)
                vec.tensor_tensor(squares[:, 0:2, :], squares[:, 0:2, :], squares[:, 6:8, :], ALU.add).then_inc(m_folded_v, 1)
                if norms[t][2] is None:
                    scale_m(t, 1)
                    update(t, 1)
                    recip(t, True, 2)
                    scale_m(t, 2)
                    update(t, 2)

            source_low(0, F - 1)
            mixer_out(0)
            norm(1)
            ffn(0)
            norm(2)

            a, v = qkv_a, qkv_v
            eng.wait_ge(h_spilled, 16 * CHUNKS * 2)
            eng.wait_ge(aux_free[1], norm_turn(1, 2, False, CHUNKS - 1) + 1)

            def head_row(j):
                return fr[0][:, j, :] if j < HEADS else fr[1][:, 2 + j - HEADS, :]

            def head_in(j):
                s = full(J_QKV + j)
                if j:
                    eng.wait_ge(a.sem, a.after(f"sq{j - 1}"))
                vec.tensor_tensor(chunked(hraw[:, :]), slots[s][:, :, 0:CW], rstd[:, :, :], ALU.mult).then_inc(main_free[s], 1)

            def head_recip(j):
                eng.wait_ge(aux_free[0], A_QKV[0] + j + 1)
                v.did(f"rec{j}", vec.reciprocal(hrstd_t[0:QW, :], hroot_t[0:QW, :]))

            def head_fin(j, c):
                turn = A_QKV[1] + j * CHUNKS + c
                eng.wait_ge(aux_full[1], turn + 1)
                if c == 0:
                    eng.wait_ge(v.sem, v.after(f"rope{j}"))
                scale = -HEAD_DIM ** -0.5 if j < HEADS else 1.0
                part = head_row(j)[:, rows[c]]
                ins = vec.scalar_tensor_tensor(out=part, in0=part, scalar=scale, in1=banks[1][:, 0:CW], op0=ALU.mult, op1=ALU.mult)
                ins.then_inc(aux_free[1], 1)

            def head_end(j):
                head_fin(j, CHUNKS - 1)
                if j >= HEADS:
                    eng.wait_ge(aux_free[1], A_QKV[1] + j * CHUNKS + CHUNKS)
                    kf = head_row(j)
                    v.did(f"dup{j}", vec.tensor_copy(kf[:, REAL:TOKENS], kf[:, 0:PAD]))
                    eng.wait_ge(khi.sem, j - HEADS + 1)
                    v.did(f"klo{j}", vec.tensor_tensor(rr[1][:, 2 + j - HEADS, :], kf, rr[1][:, j - HEADS, :].bitcast(F32),
                                                       ALU.subtract))

            def v_low(t):
                s = full(J_QKV + HN + t)
                for k in range(3):
                    tile = 3 * t + k
                    eng.wait_ge(v_hi.sem, tile + 1)
                    ins = vec.scalar_tensor_tensor(out=vlo[0:QW, tile, :], in0=slots[s][0:QW, k, 0:256],
                                                   scalar=rstd_t[0:QW, 1, tile:tile + 1],
                                                   in1=vhi[0:QW, tile, :].bitcast(F32), op0=ALU.mult, op1=ALU.subtract)
                ins.then_inc(main_free[s], 1)

            for j in range(HN + 2):
                if j < HN:
                    head_in(j)
                if j == HN:
                    v_low(0)
                if j == HN + 1:
                    v_low(1)
                if j >= 2:
                    head_end(j - 2)
                if 1 <= j <= HN:
                    head_recip(j - 1)
                if j < HN:
                    if j == 0:
                        eng.wait_ge(tables_in, 16)
                    eng.wait_ge(a.sem, a.after(f"swap{j}_3"))
                    v.did(f"cos{j}", vec.tensor_tensor(hg[:, :], hg[:, :], cossin[:, 0, :], ALU.mult))
                    v.did(f"sin{j}", vec.tensor_tensor(hs[:, :], hs[:, :], cossin[:, 1, :], ALU.mult))
                    eng.wait_ge(v.sem, v.after(f"sin{j}"))
                    v.did(f"rope{j}", vec.tensor_tensor(head_row(j), hg[:, :], hs[:, :], ALU.add))
                if 1 <= j <= HN:
                    for c in range(CHUNKS - 1):
                        head_fin(j - 1, c)
            v_low(2)

            eng.wait_ge(first_a.sem, 1)
            first_v.did("ql", vec.tensor_tensor(qsl[:, :, :], fr[0][:, :, 0:QW], qsh[:, :, :].bitcast(F32), ALU.subtract))
            first_v.did("pad", vec.memset(prob[:, :, REAL:TOKENS], 0.0))

            def row_max(k, i, did):
                slot, turn = main(J_ATT + k, i, HEADS) if not isinstance(i, int) else main(J_ATT + k + HEADS * i)
                eng.wait_ge(main_full[slot], turn + 1)
                if not (isinstance(i, int) and i == 0 and k < 2):
                    eng.wait_ge(main_free[slot], turn)
                did(vec.tensor_reduce(stat[0:QW, k % 2, 0:1], slots[slot][0:QW, :, 0:CW], mybir.AxisListType.XY, ALU.min))

            def row_sum(k, i, st, names, turn_):
                slot, turn = main(J_ATT + k, i, HEADS) if not isinstance(i, int) else main(J_ATT + k + HEADS * i)
                b = k % 2
                eng.wait_ge(main_free[slot], turn + 1)
                st.did(names[0], vec.tensor_reduce(stat[0:QW, b, 4:5], stat[0:QW, b, 1:4], AX_X, ALU.add))
                eng.wait_ge(st.sem, st.after(names[0], turn_))
                st.did(names[1], vec.reciprocal(rsum[0:QW, k % HEADS, :], stat[0:QW, b, 4:5]))

            def outputs(kv, of):
                eng.wait_ge(aux_full[1], summed(kv, of) + 1)
                k, i = (SUMS_AFTER[5], of) if kv == 0 else (SUMS_AFTER[1], of + 1) if not is_last(of) else (TURNED, of)
                eng.wait_ge(aux_free[0], turned(k, i) + 1)
                dst = fr[0][:, kv * GROUP:(kv + 1) * GROUP, bass.ds(of * QW, QW)]
                vec.tensor_tensor(dst, banks[1][:, 0:GROUP * QW].rearrange("p (h q) -> p h q", h=GROUP),
                                  recips[:, :].rearrange("p (h q) -> p h q", h=GROUP), ALU.mult).then_inc(aux_free[1], 1)

            def tile_steps(i, first=False, last=False):
                st, turn_ = (end_v, 0) if last else (att_v, i)
                for u in range(HEADS):
                    if u == 0 and not first:
                        outputs(0, i - 1)
                    if u == GROUP and not first:
                        outputs(1, i - 1)

                    def high(t):
                        eng.wait_ge(aux_free[0], turned(turned_unit(u, t), i) + 1)
                        st.did(f"hi{t}_{u}", vec.tensor_copy(PT[u // GROUP][0][0:QW, 3 * t:3 * t + 3, u % GROUP, :],
                                                             turn_f[0:QW, u % 2, t, :].rearrange("p (k q) -> p k q", k=3)))

                    high(0)
                    high(1)
                    if not last:
                        eng.wait_ge(att_a.sem, att_a.after(f"qh{u}", i))
                        st.did(f"ql{u}", vec.tensor_tensor(qsl[:, u, :], fr[0][:, u, bass.ds(i * QW + QW, QW)],
                                                           qsh[:, u, :].bitcast(F32), ALU.subtract))
                    if u + 2 < HEADS or not last:
                        row_max(u + 2, i, lambda ins: st.did(f"mx{u}", ins))
                    high(2)
                    if u + 1 < HEADS or not last:
                        row_sum(u + 1, i, st, (f"sum{u}", f"rcp{u}"), turn_)

            row_max(0, 0, lambda ins: first_v.did("mx0", ins))
            row_sum(0, 0, first_v, ("sum0", "rcp0"), 0)
            row_max(1, 0, lambda ins: first_v.did("mx1", ins))
            tile_steps(0, first=True)
            with eng.Fori(1, QT - 1) as i:
                tile_steps(i)
            tile_steps(QT - 1, last=True)
            outputs(0, QT - 1)
            for f in range(GROUP):
                source_low(1, f)
            outputs(1, QT - 1)
            for f in range(GROUP, HEADS):
                source_low(1, f)

            mixer_out(1)
            norm(3)
            ffn(1)


def unit_of(w, c0, cols=P):
    k = w.shape[0] // P
    return w[:, c0:c0 + cols].reshape(k, P, cols).transpose(1, 0, 2).reshape(P, k * cols)


def lay_out_weights(lru_w_in, lru_gate_w, lru_w_out, attn_w_qkv, attn_w_out, ffn_w_in, ffn_w_out):
    units = []
    for n in range(F):
        units.append(unit_of(lru_w_in[0], D_MODEL + n * P))
        units.append(unit_of(lru_w_in[0], n * P))
        g = lru_gate_w[0][:, :, n].reshape(4, P, P).transpose(1, 0, 2).reshape(P, 4 * P)
        units.append(np.concatenate([g, g], axis=1))
    units += [unit_of(lru_w_out[0], n * P) for n in range(F)]

    def ffn(layer):
        w_in, w_out = ffn_w_in[layer], ffn_w_out[layer]
        up = lambda r: [unit_of(w_in, r * P), unit_of(w_in, D_FF + r * P)]
        down = lambda r: [w_out[r * P:(r + 1) * P, :]]
        got = up(0) + up(1)
        for g in range(1, FF // 2):
            got += up(2 * g) + down(2 * g - 2) + down(2 * g - 1) + up(2 * g + 1)
        return got + down(FF - 2) + down(FF - 1)

    units += ffn(0)
    units += [unit_of(attn_w_qkv[0], n * P) for n in range(HEADS + KV_HEADS)]
    v0 = (HEADS + KV_HEADS) * P
    for half in range(2):
        units.append(unit_of(attn_w_qkv[0][half * 512:(half + 1) * 512], v0, KV_HEADS * P))
    units += [unit_of(attn_w_out[0], n * P) for n in range(F)]
    units += ffn(1)
    assert len(units) == UNITS
    return np.ascontiguousarray(np.stack(units))


def rope_tables():
    grid_w, pairs = 64, HEAD_DIM // 4
    inv = (np.float32(10000.0) ** (-np.arange(0, 2 * pairs, 2, dtype=np.float32) / np.float32(2 * pairs))).astype(np.float32)
    ang = np.zeros((TOKENS, 2, pairs), np.float32)
    t = np.arange(SEQ)
    ang[N_META:REAL, 0] = (t // grid_w).astype(np.float32)[:, None] * inv
    ang[N_META:REAL, 1] = (t % grid_w).astype(np.float32)[:, None] * inv
    cos, sin = np.cos(ang), np.sin(ang)
    tab = np.zeros((P, 2, TOKENS), np.float32)
    for axis in range(2):
        for half in range(2):
            at = axis * 64 + half * 32
            tab[at:at + 32, 0] = cos[:, axis].T
            tab[at:at + 32, 1] = (sin[:, axis].T if half else -sin[:, axis].T)
    return tab


def kernel(**inputs):
    import concourse.bacc as _bacc
    from concourse.bass_utils import run_bass_kernel_spmd as _run

    a = {k: np.asarray(v) for k, v in inputs.items()}
    tokens = np.concatenate([a["meta_tokens"], a["x"][0], np.zeros((PAD, D_MODEL), np.float32)], axis=0)
    h0 = np.ascontiguousarray(tokens.reshape(TOKENS, F, P).transpose(2, 1, 0))
    cols = [a["norm_gains"].reshape(8 * F, P), a["lru_conv_w"].reshape(CONV_W * F, P), a["lru_conv_b"].reshape(F, P),
            a["lru_gate_b"].reshape(4 * F, P), a["lru_lambda"].reshape(2 * F, P), a["attn_q_gain"].reshape(1, P),
            a["attn_k_gain"].reshape(1, P)]
    params = np.ascontiguousarray(np.concatenate(cols, axis=0).T)
    weights = lay_out_weights(*(a[n] for n in ("lru_w_in", "lru_gate_w", "lru_w_out", "attn_w_qkv", "attn_w_out",
                                               "ffn_w_in", "ffn_w_out")))
    arrays = {"h0_dram": h0, "params_dram": params, "rope_dram": rope_tables(), "weights_dram": weights}
    nc = _bacc.Bacc("TRN2", target_bir_lowering=False, num_devices=1)
    aps = [nc.dram_tensor(n, x.shape, F32, kind="ExternalInput").ap() for n, x in arrays.items()]
    out = nc.dram_tensor("out_dram", (P, F, TOKENS), F32, kind="ExternalOutput").ap()
    spill = nc.dram_tensor("spill_dram", (P, F, TOKENS), F32, kind="Internal").ap()
    trunk(nc, *aps, out, spill)
    r = _run(nc, [arrays], core_ids=[0])
    got = np.asarray(r.results[0]["out_dram"])
    return np.ascontiguousarray(got.transpose(2, 1, 0).reshape(TOKENS, D_MODEL)[N_META:REAL])[None]
```
